# Optimizing a Trainium2 kernel written in Bass

```python
import math
import jax, jax.numpy as jnp
from jax import lax
import numpy as np

D_MODEL = 1024
BATCH = 1
SEQ = 512
DEPTH = 2

N_A = DEPTH // 2
N_B = DEPTH - N_A
POOL_WINDOWS = (2, 4, 8, 16)
POOL_GROUPS = len(POOL_WINDOWS)
GROUP_W = D_MODEL // POOL_GROUPS
MLA_HEADS = 8
QK_NOPE = 128
QK_ROPE = 64
V_HEAD = 128
Q_RANK = 768
KV_RANK = 256
ROPE_THETA = 10000.0
ATTN_SCALE = 1.0 / math.sqrt(QK_NOPE + QK_ROPE)
Q_BLOCK = 128
PEER_HEADS = 8
N_KEYS = 128
N_EXPERTS = N_KEYS * N_KEYS
PEER_TOPK = 16
PEER_DQ = 256
PEER_DHALF = PEER_DQ // 2
TOKEN_CHUNK = 128
PLE_DIM = 256
EPS = 1e-6

kernel_name = 'yoco_pool_mla_peer_ple_trunk'

def rmsnorm(x, g):
    x32 = x.astype(jnp.float32)
    y = x32 * lax.rsqrt(jnp.mean(x32 * x32, axis=-1, keepdims=True) + EPS)
    return (y * g.astype(jnp.float32)).astype(x.dtype)

def rope_tables(positions, dtype):
    inv = ROPE_THETA ** (-jnp.arange(0, QK_ROPE, 2, dtype=jnp.float32) / QK_ROPE)
    ang = positions.astype(jnp.float32)[..., None] * inv
    return jnp.cos(ang).astype(dtype), jnp.sin(ang).astype(dtype)

def apply_rope(x, cos, sin):
    half = x.shape[-1] // 2
    x1, x2 = x[..., :half], x[..., half:]
    return jnp.concatenate([x1 * cos - x2 * sin, x2 * cos + x1 * sin], axis=-1)

def pool_mixer(h, w_groups, scale):
    B, S, D = h.shape
    h32 = h.astype(jnp.float32)
    cs = jnp.concatenate([jnp.zeros((B, 1, D), jnp.float32), jnp.cumsum(h32, axis=1)], axis=1)
    t = jnp.arange(S)
    outs = []
    for g, w in enumerate(POOL_WINDOWS):
        sl = slice(g * GROUP_W, (g + 1) * GROUP_W)
        win_sum = cs[:, 1:, sl] - cs[:, jnp.maximum(t + 1 - w, 0), sl]
        count = jnp.minimum(t + 1, w).astype(jnp.float32)[None, :, None]
        pooled = (win_sum / count - h32[..., sl]).astype(h.dtype)
        outs.append(pooled @ w_groups[g])
    return jnp.concatenate(outs, axis=-1) * scale

def shared_kv(x, kv_in_norm, w_dkv, kv_norm, w_ukv, cos, sin):
    B, S, _ = x.shape
    h = rmsnorm(x, kv_in_norm)
    ckv_kpe = h @ w_dkv
    c_kv = rmsnorm(ckv_kpe[..., :KV_RANK], kv_norm)
    k_pe = apply_rope(ckv_kpe[..., KV_RANK:], cos, sin)
    kv = (c_kv @ w_ukv).reshape(B, S, MLA_HEADS, QK_NOPE + V_HEAD)
    return kv[..., :QK_NOPE], k_pe, kv[..., QK_NOPE:]

def causal_attention(q_nope, q_pe, k_nope, k_pe, v):
    B, S, H, _ = q_nope.shape
    nb = S // Q_BLOCK
    qn = q_nope.reshape(B, nb, Q_BLOCK, H, QK_NOPE).transpose(1, 0, 2, 3, 4)
    qp = q_pe.reshape(B, nb, Q_BLOCK, H, QK_ROPE).transpose(1, 0, 2, 3, 4)
    kpos = jnp.arange(S)

    def block(args):
        qn_b, qp_b, bi = args
        s = (jnp.einsum('bqhd,bkhd->bhqk', qn_b, k_nope).astype(jnp.float32)
             + jnp.einsum('bqhr,bkr->bhqk', qp_b, k_pe).astype(jnp.float32)) * ATTN_SCALE
        qpos = bi * Q_BLOCK + jnp.arange(Q_BLOCK)
        s = jnp.where(kpos[None, :] <= qpos[:, None], s, -jnp.inf)
        pr = jax.nn.softmax(s, axis=-1).astype(v.dtype)
        return jnp.einsum('bhqk,bkhd->bqhd', pr, v)

    o = lax.map(block, (qn, qp, jnp.arange(nb)))
    return o.transpose(1, 0, 2, 3, 4).reshape(B, S, H * V_HEAD)

def mla_mixer(h, w_dq, q_norm, w_uq, w_o, k_nope, k_pe, v, cos, sin):
    B, S, _ = h.shape
    c_q = rmsnorm(h @ w_dq, q_norm)
    q = (c_q @ w_uq).reshape(B, S, MLA_HEADS, QK_NOPE + QK_ROPE)
    q_nope = q[..., :QK_NOPE]
    q_pe = apply_rope(q[..., QK_NOPE:], cos[:, :, None, :], sin[:, :, None, :])
    return causal_attention(q_nope, q_pe, k_nope, k_pe, v) @ w_o

def peer_mixer(h, w_q, sub_keys, u, v):
    B, S, D = h.shape
    q = (h @ w_q).astype(jnp.float32).reshape(B, S, PEER_HEADS, 2, PEER_DHALF)
    s = jnp.einsum('bshpc,hpnc->bshpn', q, sub_keys.astype(jnp.float32))
    top_s, top_i = lax.top_k(s, PEER_TOPK)
    cand_s = (top_s[..., 0, :, None] + top_s[..., 1, None, :]).reshape(B, S, PEER_HEADS, PEER_TOPK * PEER_TOPK)
    cand_i = (top_i[..., 0, :, None] * N_KEYS + top_i[..., 1, None, :]).reshape(B, S, PEER_HEADS, PEER_TOPK * PEER_TOPK)
    best_s, pos = lax.top_k(cand_s, PEER_TOPK)
    idx = jnp.take_along_axis(cand_i, pos, axis=-1)
    gate = jax.nn.softmax(best_s, axis=-1)
    n_chunks = (B * S) // TOKEN_CHUNK
    hc = h.reshape(n_chunks, TOKEN_CHUNK, D)
    ic = idx.reshape(n_chunks, TOKEN_CHUNK, PEER_HEADS * PEER_TOPK)
    gc = gate.reshape(n_chunks, TOKEN_CHUNK, PEER_HEADS * PEER_TOPK).astype(h.dtype)

    def chunk(args):
        hh, ii, gg = args
        a = jnp.einsum('tkd,td->tk', u[ii], hh)
        w = gg * jax.nn.gelu(a)
        return jnp.einsum('tk,tkd->td', w, v[ii])

    return lax.map(chunk, (hc, ic, gc)).reshape(B, S, D)

def setup_inputs(seed: int = 0) -> dict:
    key = jax.random.key(seed)
    ks = jax.random.split(key, 24)
    f32 = jnp.float32

    def nrm(k, shape, fan_in):
        return jax.random.normal(k, shape, f32) * (fan_in ** -0.5)

    def gain(k, shape):
        return 1.0 + 0.02 * jax.random.normal(k, shape, f32)

    D = D_MODEL
    return {
        'x': jax.random.normal(ks[0], (BATCH, SEQ, D), f32),
        'p': jax.random.normal(ks[1], (DEPTH, BATCH, SEQ, PLE_DIM), f32),
        'positions': jax.random.randint(ks[2], (BATCH, 1), 0, 1024, jnp.int32) + jnp.arange(SEQ, dtype=jnp.int32)[None, :],
        'mix_norm': gain(ks[3], (DEPTH, D)),
        'ffn_norm': gain(ks[4], (DEPTH, D)),
        'pool_w': nrm(ks[5], (N_A, POOL_GROUPS, GROUP_W, GROUP_W), GROUP_W),
        'pool_scale': gain(ks[6], (N_A, D)),
        'kv_in_norm': gain(ks[7], (D,)),
        'w_dkv': nrm(ks[8], (D, KV_RANK + QK_ROPE), D),
        'kv_norm': gain(ks[9], (KV_RANK,)),
        'w_ukv': nrm(ks[10], (KV_RANK, MLA_HEADS * (QK_NOPE + V_HEAD)), KV_RANK),
        'w_dq': nrm(ks[11], (N_B, D, Q_RANK), D),
        'q_norm': gain(ks[12], (N_B, Q_RANK)),
        'w_uq': nrm(ks[13], (N_B, Q_RANK, MLA_HEADS * (QK_NOPE + QK_ROPE)), Q_RANK),
        'w_o': nrm(ks[14], (N_B, MLA_HEADS * V_HEAD, D), MLA_HEADS * V_HEAD),
        'peer_wq': nrm(ks[15], (DEPTH, D, PEER_HEADS * PEER_DQ), D),
        'peer_keys': nrm(ks[16], (DEPTH, PEER_HEADS, 2, N_KEYS, PEER_DHALF), PEER_DHALF),
        'peer_u': nrm(ks[17], (DEPTH, N_EXPERTS, D), D),
        'peer_v': nrm(ks[18], (DEPTH, N_EXPERTS, D), PEER_HEADS),
        'ple_norm': gain(ks[19], (DEPTH, D)),
        'ple_wg': nrm(ks[20], (DEPTH, D, D), D),
        'ple_wp': nrm(ks[21], (DEPTH, PLE_DIM, D), PLE_DIM),
        'final_norm': gain(ks[22], (D,)),
    }

def reference(x, p, positions, mix_norm, ffn_norm, pool_w, pool_scale, kv_in_norm, w_dkv, kv_norm, w_ukv,
              w_dq, q_norm, w_uq, w_o, peer_wq, peer_keys, peer_u, peer_v, ple_norm, ple_wg, ple_wp, final_norm):
    cos, sin = rope_tables(positions, x.dtype)
    k_nope = k_pe = v_sh = None
    for i in range(DEPTH):
        h = rmsnorm(x, mix_norm[i])
        if i < N_A:
            x = x + pool_mixer(h, pool_w[i], pool_scale[i])
        else:
            if i == N_A:
                k_nope, k_pe, v_sh = shared_kv(x, kv_in_norm, w_dkv, kv_norm, w_ukv, cos, sin)
            j = i - N_A
            x = x + mla_mixer(h, w_dq[j], q_norm[j], w_uq[j], w_o[j], k_nope, k_pe, v_sh, cos, sin)
        x = x + peer_mixer(rmsnorm(x, ffn_norm[i]), peer_wq[i], peer_keys[i], peer_u[i], peer_v[i])
        g = jax.nn.sigmoid((rmsnorm(x, ple_norm[i]) @ ple_wg[i]).astype(jnp.float32)).astype(x.dtype)
        x = x + g * (p[i] @ ple_wp[i])
    return rmsnorm(x, final_norm)


_drawn_inputs = setup_inputs


def setup_inputs(seed=0):
    import zlib

    import numpy as np

    out = dict(_drawn_inputs(seed))
    spreads = {}
    factors = {'kv_in_norm': 8.0, 'kv_norm': 7.98, 'q_norm': 8.0, 'ple_norm': 7.437, 'final_norm': 2.819}
    for name, (base, spread) in spreads.items():
        noise = np.random.default_rng([zlib.crc32(name.encode()), seed]).standard_normal(out[name].shape)
        drawn = base * np.exp(spread * noise) if base else spread * noise
        out[name] = __import__('jax').numpy.asarray(drawn.astype(out[name].dtype))
    for name, factor in factors.items():
        out[name] = (out[name] * factor).astype(out[name].dtype)
    return out
```

```python
import numpy as np
import concourse.bass as bass
from concourse import mybir
from contextlib import ExitStack

F32 = mybir.dt.float32
BF16 = mybir.dt.bfloat16
I32 = mybir.dt.int32
U32 = mybir.dt.uint32
ALU = mybir.AluOpType
ACT = mybir.ActivationFunctionType
AX = mybir.AxisListType.X

P = 128
S, D, DEPTH = 512, 1024, 2
NC = S // P
DB = D // P
PAIRS = DEPTH * NC
WINDOWS = (2, 4, 8, 16)
GW = D // len(WINDOWS)
H, NOPE, ROPE, VH = 8, 128, 64, 128
HALF = ROPE // 2
QR, KVR = 768, 256
SCALE = 1.0 / float(np.sqrt(NOPE + ROPE))
PH, TOPK = 8, 16
KSEL = PH * TOPK
NEXP = P * P
PLE = 256
EPS = 1e-6
LOW = -3.0e38

RING = 3
PIECE = 2048
SLOTS = 8
BATCH = 4
SEGMENTS = 8
LOOPS = KSEL // SLOTS // SEGMENTS

C_IDENT, C_MASK, C_IOTA, C_INV, C_EPS = 0, P, 2 * P, 2 * P + TOPK, 2 * P + TOPK + HALF
C_WIDTH = C_EPS + 1
G_KV, G_MIX1, G_PLE, G_CKV, G_Q = 0, DB, 2 * DB, 4 * DB, 4 * DB + KVR // P
G_WIDTH = G_Q + QR // P

FRONT = (["pool", "query", "score", "pick", "select"],
         ["latent", "keys", "queries", "heads0", "heads1", "project", "query", "score", "pick", "select"])
BACK = ["residual", "embed"]

USES = {"pool": [("pool_w", 1)], "query": [("wq", 8)], "score": [("keys", 1)],
        "latent": [("w_dkv", 2)], "keys": [("w_ukv_k", 1), ("w_ukv_v", 1), ("w_dq", 3)],
        "queries": [("w_uq_nope", 4), ("w_uq_pe", 2)], "project": [("w_o", 4)],
        "embed": [("ple_wg", 4), ("ple_wp", 1)]}

INCS = {
    "pool": dict(normed=1, t_filled=1, t_copied=1, x_ready=1),
    "query": dict(normed=1, hp_ready=1, t_filled=1, t_copied=1, s_copied=4),
    "score": dict(m_filled=3, m_copied=4),
    "latent": dict(normed=2, hat_ready=1, t_filled=2, t_copied=2, m_copied=1),
    "keys": dict(normed=1, s_copied=1, m_copied=2),
    "queries": dict(t_filled=2, t_copied=2, s_copied=1, m_copied=1),
    "heads0": dict(m_copied=1),
    "heads1": dict(m_copied=1),
    "project": dict(x_ready=1),
    "residual": dict(normed=1, x_ready=1, hat_ready=1, t_filled=1, t_copied=1),
    "embed": dict(m_copied=1, s_copied=1, x_ready=1),
    "embed1": dict(m_copied=1, s_copied=1, x_ready=1, normed=1),
}


def front(g):
    return [(s, g) for s in FRONT[g // NC]]


def back(g):
    return [(s, g) for s in BACK]


def between(g):
    return (back(g - 1) if g else []) + (front(g + 1) if g + 1 < PAIRS else [])


def segment_stages(g, j):
    b = between(g)
    n = SEGMENTS - 1
    return [st for i, st in enumerate(b) if i * n // len(b) == j]


SCHEDULE = front(0) + [st for g in range(PAIRS) for st in between(g)] + back(PAIRS - 1)


def incs(stage, g):
    return INCS.get("embed1" if stage == "embed" and g >= NC else stage, {})


def totals():
    count, at = {}, {}
    for stage, g in SCHEDULE:
        at[stage, g] = dict(count)
        for name, n in incs(stage, g).items():
            count[name] = count.get(name, 0) + n
    return at


AT = totals()


def before(name, stage, g):
    return AT[stage, g].get(name, 0)


def after(name, stage, g):
    return before(name, stage, g) + incs(stage, g).get(name, 0)


PIECES = {}
for _stage, _g in SCHEDULE:
    for _w, _n in USES.get(_stage, []):
        for _i in range(_n):
            PIECES[_w, _g, _i] = len(PIECES)

NORMS = sum(incs(s_, g_).get("normed", 0) for s_, g_ in SCHEDULE)


def trunk(nc, consts, pools, gcols, gains, positions, x, pT, uv, weights, out):
    ctx = ExitStack()
    with ctx:
        def sb(name, shape, dt=F32):
            return ctx.enter_context(nc.sbuf_tensor(name, shape, dt))

        def sem(name):
            return ctx.enter_context(nc.semaphore(name))

        X = sb("X", [P, NC, D])
        KV = sb("KV", [P, 2 * NC * D])
        KT = KV[:, 0:NC * D].rearrange("p (h s) -> p h s", h=H)
        V = KV[:, NC * D:2 * NC * D].rearrange("p (c d) -> p c d", c=NC)
        poolm = KV[:, 0:12 * P].rearrange("p (k w t) -> p k w t", k=3, w=4)
        mix_gain = KV[:, 12 * P:12 * P + D]
        pool_scale = KV[:, 12 * P + D:12 * P + 2 * D]
        KPE = sb("KPE", [ROPE, S])
        cs = sb("cs", [P, 2, NC, HALF])
        cst = sb("cst", [P, C_WIDTH])
        gc = sb("gc", [P, G_WIDTH])
        ffn_gain = sb("ffn_gain", [P, D])
        final_gain = sb("final_gain", [P, D])
        HP = sb("HP", [P, 2, D])
        A = sb("A", [P, 2, D])
        TT = sb("TT", [P, DB, P])
        TU = sb("TU", [P, D])
        SC = sb("SC", [P, PIECE])
        SD = sb("SD", [P, PIECE])
        sq_out = sb("sq_out", [P, D], BF16)
        ring = [sb(f"w{i}", [P, PIECE]) for i in range(RING)]
        pt = sb("pt", [P, 2, PLE // P, P])
        ss = sb("ss", [P, NORMS])
        rms = sb("rms", [P, NORMS])
        rstd = sb("rstd", [P, NORMS])
        slot = [sb(f"slot{i}", [P, 2 * D]) for i in range(SLOTS)]
        diag = [sb(f"diag{i}", [P, P]) for i in range(SLOTS)]
        a = sb("a", [P, SLOTS])
        act_a = sb("act_a", [P, SLOTS])
        w = sb("w", [P, SLOTS])
        idx = sb("idx", [P, 2, KSEL], I32)
        gate = sb("gate", [P, 2, KSEL])
        top = sb("top", [P, PH, 2, TOPK])
        top_u = sb("top_u", [P, PH, 2, TOPK], U32)
        top_i = sb("top_i", [P, PH, 2, TOPK])
        best = sb("best", [P, PH, TOPK])
        pos_u = sb("pos_u", [P, PH, TOPK], U32)
        half_u = sb("half_u", [P, 2, KSEL], U32)
        half_f = sb("half_f", [P, 2, KSEL])
        sel = sb("sel", [P, 2, KSEL])
        shifted = sb("shifted", [P, PH, TOPK])
        gsum = sb("gsum", [P, PH])
        grec = sb("grec", [P, PH])
        amax = sb("amax", [P, NC * H])
        nmax = sb("nmax", [P, NC * H])
        asum = sb("asum", [P, NC * H])
        arec = sb("arec", [P, NC * H])
        pos_i = sb("pos_i", [P, NC], I32)
        pos_f = sb("pos_f", [P, NC])
        zeros = sb("zeros", [P, P])

        ident = cst[:, C_IDENT:C_IDENT + P]
        mask = cst[:, C_MASK:C_MASK + P]
        iota = cst[:, C_IOTA:C_IOTA + TOPK]
        inv = cst[:, C_INV:C_INV + HALF]
        eps = cst[:, C_EPS:C_EPS + 1]

        def ps(name, width):
            return ctx.enter_context(nc.psum_tensor(name, [P, width], F32))

        acc = ps("acc", D)
        M = ps("M", D)
        T = ps("T", D)
        B = ps("B", D)
        blocks = "p (b t) -> p b t"

        Q16 = SD[:, :].rearrange(blocks, t=P)
        scores = SC[:, :].rearrange(blocks, t=P)
        rest = SD[:, :].rearrange(blocks, t=P)
        ckv, kpe, ckvT = SD[:, 0:KVR], SD[:, KVR:KVR + ROPE], SD[:, 512:512 + KVR]
        qpe, rtmp = SD[:, 1024:1024 + H * ROPE], SD[:, 1536:2048]
        QT = A[:, 0, :].rearrange(blocks, t=P)
        QPT = TU[0:ROPE, :].rearrange(blocks, t=P)
        prob = [SC[:, 512 * i:512 * i + 512] for i in range(2)]
        probT = [SC[:, 1024 + 512 * i:1536 + 512 * i] for i in range(2)]

        const_loaded = sem("const_loaded")
        x_loaded = [sem(f"x_loaded{c}") for c in range(NC)]
        w_loaded = [sem(f"w_loaded{i}") for i in range(RING)]
        pt_loaded = [sem(f"pt_loaded{i}") for i in range(2)]
        gain_loaded = sem("gain_loaded")
        weights_used = sem("weights_used")
        names = ["normed", "hat_ready", "hp_ready", "x_ready", "t_filled", "t_copied", "m_filled",
                 "m_copied", "s_copied"]
        sems = {n: sem(n) for n in names}
        normed, hat_ready, hp_ready, x_ready = (sems[n] for n in names[:4])
        t_filled, t_copied, m_filled, m_copied, s_copied = (sems[n] for n in names[4:])
        squared = sem("squared")
        mixed = sem("mixed")
        att_scored, att_maxed, att_exped = sem("att_scored"), sem("att_maxed"), sem("att_exped")
        att_normed, att_turned, att_copied, att_out = (sem("att_normed"), sem("att_turned"),
                                                       sem("att_copied"), sem("att_out"))
        gate_shifted, gate_exped = sem("gate_shifted"), sem("gate_exped")
        idx_ready = sem("idx_ready")
        rows_loaded = [sem(f"rows_loaded{i}") for i in range(SLOTS)]
        slots_free, dotted, gelued, weighted, diag_ready = (sem("slots_free"), sem("dotted"), sem("gelued"),
                                                            sem("weighted"), sem("diag_ready"))
        acc_done = sem("acc_done")
        out_ready, out_stored = sem("out_ready"), sem("out_stored")
        dve_steps = sem("dve_steps")
        trig_shifted, trig_done = sem("trig_shifted"), sem("trig_done")
        zeroed = sem("zeroed")

        def used(name, g, i):
            return PIECES[name, g, i] + 1

        def norm_number(stage, g, i=0):
            return before("normed", stage, g) + i

        CONSTS = 8
        block = ctx.enter_context(nc.Block())

        @block.sync
        def _(sp):
            sp.dma_start(X[:, 0, :], x[0:P, :]).then_inc(x_loaded[0], 16)
            sp.dma_start(cst[:], consts).then_inc(const_loaded, 16)
            sp.dma_start(KV[:, 0:12 * P], pools).then_inc(const_loaded, 16)
            sp.dma_start(mix_gain, gains[0:1, :].broadcast_to([P, D])).then_inc(const_loaded, 16)
            sp.dma_start(pool_scale, gains[1:2, :].broadcast_to([P, D])).then_inc(const_loaded, 16)
            sp.dma_start(ffn_gain[:], gains[2:3, :].broadcast_to([P, D])).then_inc(const_loaded, 16)
            sp.dma_start(gc[:], gcols).then_inc(const_loaded, 16)
            sp.dma_start(pos_i[:], positions).then_inc(const_loaded, 16)
            sp.dma_start(final_gain[:], gains[4:5, :].broadcast_to([P, D])).then_inc(const_loaded, 16)
            chunks = 1
            for (name, g, i), n in PIECES.items():
                if name == "ple_wp":
                    if g >= 2:
                        sp.wait_ge(weights_used, used("ple_wp", g - 2, 0))
                    sp.dma_start(pt[:, g % 2], pT[g // NC, :, :, (g % NC) * P:(g % NC) * P + P]
                                 ).then_inc(pt_loaded[g % 2], 16)
                if n >= RING:
                    sp.wait_ge(weights_used, n - RING + 1)
                src = weights[name, g // NC][i]
                sp.dma_start(ring[n % RING][:, 0:src.shape[1]], src).then_inc(w_loaded[n % RING], 16)
                if chunks < NC and n >= RING - 1:
                    sp.dma_start(X[:, chunks, :], x[chunks * P:chunks * P + P, :]).then_inc(x_loaded[chunks], 16)
                    chunks += 1
                if (name, g, i) == ("wq", NC - 1, 7):
                    sp.wait_ge(hp_ready, after("hp_ready", "query", NC - 1))
                    sp.dma_start(ffn_gain[:], gains[3:4, :].broadcast_to([P, D])).then_inc(gain_loaded, 16)

        @block.gpsimd
        def _(pool):
            for g in range(PAIRS):
                pool.wait_ge(idx_ready, g + 1)
                for k in range(KSEL):
                    pool.wait_ge(slots_free, g * KSEL + k + 1)
                    nc.gpsimd.indirect_dma_start(
                        out=slot[k % SLOTS][:], out_offset=None, in_=uv[g // NC],
                        in_offset=bass.IndirectOffsetOnAxis(ap=idx[:, g % 2, k:k + 1], axis=0),
                    ).then_inc(rows_loaded[k % SLOTS], 16)

        @block.tensor
        def _(pe):
            def piece(name, g, i):
                n = PIECES[name, g, i]
                pe.wait_ge(w_loaded[n % RING], 16 * (n // RING + 1))
                return ring[n % RING]

            def transposes(stage, g, src, n, width=P):
                for b in range(n):
                    last = nc.tensor.transpose(T[0:width, b * P:(b + 1) * P], src[:, b * width:(b + 1) * width],
                                               ident)
                return last

            def token_major(dst, lhsT, wp, kb, cols):
                for k in range(kb):
                    last = nc.tensor.matmul(dst, lhsT[:, k, :], wp[:, k * cols:(k + 1) * cols],
                                            start=(k == 0), stop=(k == kb - 1))
                return last

            def pool_stage(g):
                pe.wait_ge(mixed, g + 1)
                if g:
                    pe.wait_ge(t_copied, before("t_copied", "pool", g))
                for b in range(DB):
                    wnd = b // 2
                    dst = T[:, b * P:(b + 1) * P]
                    if g:
                        nc.tensor.matmul(dst, A[:, (g - 1) % 2, b * P:(b + 1) * P], poolm[:, 2, wnd, :],
                                         start=True, stop=False)
                    last = nc.tensor.matmul(dst, A[:, g % 2, b * P:(b + 1) * P], poolm[:, 1 if g else 0, wnd, :],
                                            start=(g == 0), stop=True)
                last.then_inc(t_filled, 1)
                pe.wait_ge(t_copied, after("t_copied", "pool", g))
                wp = piece("pool_w", g, 0)
                for wnd in range(len(WINDOWS)):
                    last = token_major(M[:, wnd * GW:(wnd + 1) * GW], TT[:, 2 * wnd:2 * wnd + 2, :],
                                       wp[:, 512 * wnd:512 * wnd + 512], 2, GW)
                last.then_inc(weights_used, 1)

            def query_stage(g):
                pe.wait_ge(hp_ready, after("hp_ready", "query", g))
                pe.wait_ge(t_copied, before("t_copied", "query", g))
                transposes("query", g, HP[:, g % 2, :], DB).then_inc(t_filled, 1)
                pe.wait_ge(t_copied, after("t_copied", "query", g))
                for b in range(4):
                    if before("s_copied", "query", g) or b > 1:
                        pe.wait_ge(s_copied, before("s_copied", "query", g) + max(b - 1, 0))
                    for j in range(2):
                        wp = piece("wq", g, 2 * b + j)
                        for q in range(2):
                            dst = B[:, (b % 2) * 512 + (2 * j + q) * P:(b % 2) * 512 + (2 * j + q + 1) * P]
                            for k in range(DB):
                                last = nc.tensor.matmul(dst, wp[:, k * 256 + q * P:k * 256 + (q + 1) * P],
                                                        TT[:, k, :], start=(k == 0), stop=(k == DB - 1))
                        last.then_inc(weights_used, 1)

            def score_stage(g):
                wp = piece("keys", g, 0)
                for b in range(4):
                    pe.wait_ge(s_copied, after("s_copied", "query", g) - 3 + b)
                    if b > 1 or before("m_copied", "score", g):
                        pe.wait_ge(m_copied, before("m_copied", "score", g) + max(b - 1, 0))
                    for q in range(4):
                        hp = 4 * b + q
                        last = nc.tensor.matmul(M[:, (b % 2) * 512 + q * P:(b % 2) * 512 + (q + 1) * P],
                                                Q16[:, hp, :], wp[:, hp * P:(hp + 1) * P], start=True, stop=True)
                    if b < 3:
                        last.then_inc(m_filled, 1)
                last.then_inc(weights_used, 1)

            def latent_stage(g):
                pe.wait_ge(hat_ready, after("hat_ready", "latent", g))
                pe.wait_ge(t_copied, before("t_copied", "latent", g))
                transposes("latent", g, A[:, 0, :], DB).then_inc(t_filled, 1)
                pe.wait_ge(t_copied, before("t_copied", "latent", g) + 1)
                pe.wait_ge(m_copied, before("m_copied", "latent", g))
                kvT = TU[:, :].rearrange(blocks, t=P)
                token_major(M[:, 0:KVR], kvT, piece("w_dkv", g, 0), DB, KVR).then_inc(weights_used, 1)
                token_major(M[:, 512:512 + ROPE], kvT, piece("w_dkv", g, 1), DB, ROPE).then_inc(weights_used, 1)
                pe.wait_ge(m_copied, after("m_copied", "latent", g))
                transposes("latent", g, ckv, 2)
                nc.tensor.transpose(T[0:ROPE, 2 * P:3 * P], kpe, ident).then_inc(t_filled, 1)

            def keys_stage(g):
                pe.wait_ge(t_copied, after("t_copied", "latent", g))
                pe.wait_ge(s_copied, before("s_copied", "keys", g))
                wp = piece("w_ukv_k", g, 0)
                for h in range(H):
                    for k in range(2):
                        last = nc.tensor.matmul(B[:, h * P:(h + 1) * P], wp[:, k * 1024 + h * P:k * 1024 + (h + 1) * P],
                                                ckvT[:, k * P:(k + 1) * P], start=(k == 0), stop=(k == 1))
                last.then_inc(weights_used, 1)
                wp = piece("w_ukv_v", g, 0)
                for half in range(2):
                    for k in range(2):
                        last = nc.tensor.matmul(M[:, half * 512:half * 512 + 512], ckvT[:, k * P:(k + 1) * P],
                                                wp[:, k * 1024 + half * 512:k * 1024 + half * 512 + 512],
                                                start=(k == 0), stop=(k == 1))
                last.then_inc(weights_used, 1)
                pe.wait_ge(m_copied, before("m_copied", "keys", g) + 1)
                for i in range(3):
                    token_major(M[:, i * 256:(i + 1) * 256], TT, piece("w_dq", g, i), DB, 256).then_inc(weights_used, 1)

            def queries_stage(g):
                pe.wait_ge(m_copied, after("m_copied", "keys", g))
                transposes("queries", g, A[:, 1, :], QR // P).then_inc(t_filled, 1)
                pe.wait_ge(t_copied, before("t_copied", "queries", g) + 1)
                pe.wait_ge(s_copied, before("s_copied", "queries", g))
                for i in range(4):
                    wp = piece("w_uq_nope", g, i)
                    for q in range(2):
                        dst = B[:, (2 * i + q) * P:(2 * i + q + 1) * P]
                        for k in range(QR // P):
                            last = nc.tensor.matmul(dst, wp[:, k * 256 + q * P:k * 256 + (q + 1) * P], TT[:, k, :],
                                                    start=(k == 0), stop=(k == QR // P - 1))
                    last.then_inc(weights_used, 1)
                for i in range(2):
                    token_major(M[:, i * 256:(i + 1) * 256], TT, piece("w_uq_pe", g, i), QR // P, 256
                                ).then_inc(weights_used, 1)
                pe.wait_ge(m_copied, after("m_copied", "queries", g))
                transposes("queries", g, qpe, H, ROPE).then_inc(t_filled, 1)
                pe.wait_ge(t_copied, after("t_copied", "queries", g))

            def att_score(g, h):
                c, n = g % NC, (g % NC) * H + h
                if h < 2:
                    pe.wait_ge(s_copied, after("s_copied", "queries", g))
                else:
                    pe.wait_ge(att_exped, n - 1)
                dst = B[:, (h % 2) * 512:(h % 2) * 512 + (c + 1) * P]
                nc.tensor.matmul(dst, QT[:, h, :], KT[:, h, 0:(c + 1) * P], start=True, stop=False)
                nc.tensor.matmul(dst, QPT[:, h, :], KPE[:, 0:(c + 1) * P], start=False, stop=True
                                 ).then_inc(att_scored, 1)

            def heads_stage(g, first):
                c = g % NC
                if first == 0:
                    att_score(g, 0)
                    att_score(g, 1)
                for h in range(first, first + 4):
                    n = c * H + h
                    pe.wait_ge(att_normed, n + 1)
                    if h >= 2:
                        pe.wait_ge(att_copied, n - 1)
                    for b in range(c + 1):
                        last = nc.tensor.transpose(T[:, (h % 2) * 512 + b * P:(h % 2) * 512 + (b + 1) * P],
                                                   prob[h % 2][:, b * P:(b + 1) * P], ident)
                    last.then_inc(att_turned, 1)
                    if h + 2 < H:
                        att_score(g, h + 2)
                    pe.wait_ge(att_copied, n + 1)
                    for b in range(c + 1):
                        last = nc.tensor.matmul(M[:, h * P:(h + 1) * P], V[:, b, h * P:(h + 1) * P],
                                                probT[h % 2][:, b * P:(b + 1) * P], start=(b == 0), stop=(b == c))
                    last.then_inc(att_out, 1)

            def project_stage(g):
                pe.wait_ge(m_copied, after("m_copied", "heads1", g))
                for i in range(4):
                    token_major(M[:, i * 256:(i + 1) * 256], TT, piece("w_o", g, i), DB, 256).then_inc(weights_used, 1)

            def residual_stage(g):
                pe.wait_ge(hat_ready, after("hat_ready", "residual", g))
                pe.wait_ge(t_copied, before("t_copied", "residual", g))
                transposes("residual", g, TU, DB).then_inc(t_filled, 1)

            def embed_stage(g):
                pe.wait_ge(t_copied, after("t_copied", "residual", g))
                pe.wait_ge(m_copied, before("m_copied", "embed", g))
                for i in range(4):
                    token_major(M[:, i * 256:(i + 1) * 256], TT, piece("ple_wg", g, i), DB, 256
                                ).then_inc(weights_used, 1)
                pe.wait_ge(pt_loaded[g % 2], 16 * (g // 2 + 1))
                pe.wait_ge(s_copied, before("s_copied", "embed", g))
                wp = piece("ple_wp", g, 0)
                for half in range(2):
                    for k in range(2):
                        last = nc.tensor.matmul(B[:, half * 512:half * 512 + 512], pt[:, g % 2, k, :],
                                                wp[:, k * 1024 + half * 512:k * 1024 + half * 512 + 512],
                                                start=(k == 0), stop=(k == 1))
                last.then_inc(weights_used, 1)

            stages = dict(pool=pool_stage, query=query_stage, score=score_stage, latent=latent_stage,
                          keys=keys_stage, queries=queries_stage, heads0=lambda g: heads_stage(g, 0),
                          heads1=lambda g: heads_stage(g, 4), project=project_stage,
                          residual=residual_stage, embed=embed_stage)

            def gather_segment(g, j):
                base = g * KSEL + j * LOOPS * SLOTS
                with pe.Fori(0, LOOPS) as it:
                    for s in range(SLOTS):
                        pe.wait_ge(diag_ready, it * SLOTS + (base + s + 1))
                        for half in range(2):
                            last = nc.tensor.matmul(acc[:, half * 512:half * 512 + 512], diag[s][:],
                                                    slot[s][:, D + half * 512:D + half * 512 + 512],
                                                    start=False, stop=False)
                        last.then_inc(slots_free, 1)

            pe.wait_ge(const_loaded, 16 * CONSTS)
            pe.wait_ge(zeroed, 1)
            for stage, g in front(0):
                if stage in stages:
                    stages[stage](g)
            for g in range(PAIRS):
                if g:
                    pe.wait_ge(x_ready, after("x_ready", "residual", g - 1))
                for half in range(2):
                    last = nc.tensor.matmul(acc[:, half * 512:half * 512 + 512], zeros[:], HP[:, g % 2, 0:512],
                                            start=True, stop=False)
                if g == 0:
                    last.then_inc(slots_free, SLOTS)
                for j in range(SEGMENTS):
                    for stage, gg in segment_stages(g, j):
                        if stage in stages:
                            stages[stage](gg)
                    gather_segment(g, j)
                for half in range(2):
                    last = nc.tensor.matmul(acc[:, half * 512:half * 512 + 512], zeros[:], HP[:, g % 2, 0:512],
                                            start=False, stop=True)
                last.then_inc(acc_done, 1)
            for stage, g in back(PAIRS - 1):
                stages[stage](g)

        @block.scalar
        def _(act):
            def norm(stage, g, src, width, i=0):
                n = norm_number(stage, g, i)
                nc.scalar.activation(sq_out[:, 0:width], src, ACT.Square, accum_out=ss[:, n:n + 1]
                                     ).then_inc(squared, 1)
                act.wait_ge(squared, n + 1)
                nc.scalar.activation(rms[:, n:n + 1], ss[:, n:n + 1], ACT.Sqrt, bias=eps, scale=1.0 / width
                                     ).then_inc(normed, 1)

            def pool_stage(g):
                act.wait_ge(x_loaded[g], 16)
                norm("pool", g, X[:, g, :], D)
                act.wait_ge(t_filled, after("t_filled", "pool", g))
                nc.scalar.activation(TT[:, :, :], T[:, :].rearrange(blocks, t=P), ACT.Copy).then_inc(t_copied, 1)

            def query_stage(g):
                act.wait_ge(x_ready, before("x_ready", "query", g))
                norm("query", g, X[:, g % NC, :], D)
                act.wait_ge(t_filled, after("t_filled", "query", g))
                nc.scalar.activation(TT[:, :, :], T[:, :].rearrange(blocks, t=P), ACT.Copy).then_inc(t_copied, 1)
                if g:
                    act.wait_ge(idx_ready, g)
                for b in range(4):
                    act.wait_ge(weights_used, used("wq", g, 2 * b + 1))
                    nc.scalar.activation(SD[:, b * 512:(b + 1) * 512], B[:, (b % 2) * 512:(b % 2) * 512 + 512],
                                         ACT.Copy).then_inc(s_copied, 1)

            def score_stage(g):
                for b in range(4):
                    if b < 3:
                        act.wait_ge(m_filled, before("m_filled", "score", g) + b + 1)
                    else:
                        act.wait_ge(weights_used, used("keys", g, 0))
                    nc.scalar.activation(SC[:, b * 512:(b + 1) * 512], M[:, (b % 2) * 512:(b % 2) * 512 + 512],
                                         ACT.Copy).then_inc(m_copied, 1)

            def select_stage(g):
                act.wait_ge(gate_shifted, g + 1)
                nc.scalar.activation(shifted[:, :, :], shifted[:, :, :], ACT.Exp).then_inc(gate_exped, 1)

            def latent_stage(g):
                act.wait_ge(x_ready, before("x_ready", "latent", g))
                norm("latent", g, X[:, g % NC, :], D)
                act.wait_ge(weights_used, used("w_dkv", g, 0))
                norm("latent", g, M[:, 0:KVR], KVR, 1)

            def keys_stage(g):
                c = g % NC
                act.wait_ge(weights_used, used("w_ukv_k", g, 0))
                nc.scalar.activation(KT[:, :, c * P:(c + 1) * P], B[:, :].rearrange(blocks, t=P), ACT.Copy
                                     ).then_inc(s_copied, 1)
                act.wait_ge(weights_used, used("w_ukv_v", g, 0))
                nc.scalar.activation(V[:, c, :], M[:, :], ACT.Copy).then_inc(m_copied, 1)
                act.wait_ge(weights_used, used("w_dq", g, 2))
                norm("keys", g, M[:, 0:QR], QR)

            def queries_stage(g):
                act.wait_ge(weights_used, used("w_uq_nope", g, 3))
                nc.scalar.activation(QT, B[:, :].rearrange(blocks, t=P), ACT.Copy).then_inc(s_copied, 1)
                act.wait_ge(t_filled, after("t_filled", "queries", g))
                nc.scalar.activation(QPT, T[0:ROPE, :].rearrange(blocks, t=P), ACT.Copy).then_inc(t_copied, 1)

            def heads_stage(g, first):
                c = g % NC
                width = (c + 1) * P

                def exp(h):
                    n = c * H + h
                    act.wait_ge(att_maxed, n + 1)
                    nc.scalar.activation(prob[h % 2][:, 0:width], B[:, (h % 2) * 512:(h % 2) * 512 + width], ACT.Exp,
                                         bias=nmax[:, n:n + 1], scale=SCALE, accum_out=asum[:, n:n + 1]
                                         ).then_inc(att_exped, 1)

                if first == 0:
                    exp(0)
                    exp(1)
                for h in range(first, first + 4):
                    n = c * H + h
                    act.wait_ge(att_turned, n + 1)
                    nc.scalar.activation(probT[h % 2][:, 0:width], T[:, (h % 2) * 512:(h % 2) * 512 + width], ACT.Copy
                                         ).then_inc(att_copied, 1)
                    if h + 2 < H:
                        exp(h + 2)
                act.wait_ge(att_out, c * H + first + 4)
                nc.scalar.activation(TT[:, first:first + 4, :], M[:, first * P:(first + 4) * P].rearrange(blocks, t=P),
                                     ACT.Copy).then_inc(m_copied, 1)

            def residual_stage(g):
                act.wait_ge(x_ready, after("x_ready", "residual", g))
                norm("residual", g, X[:, g % NC, :], D)

            def embed_stage(g):
                act.wait_ge(weights_used, used("ple_wg", g, 3))
                nc.scalar.activation(TU[:, :], M[:, :], ACT.Sigmoid).then_inc(m_copied, 1)
                if g >= NC:
                    act.wait_ge(x_ready, after("x_ready", "embed", g))
                    norm("embed", g, X[:, g % NC, :], D)
                    act.wait_ge(out_ready, g - NC + 1)
                    act.dma_start(out[(g - NC) * P:(g - NC + 1) * P, :], HP[:, g % 2, :]).then_inc(out_stored, 16)

            stages = dict(pool=pool_stage, query=query_stage, score=score_stage, select=select_stage,
                          latent=latent_stage, keys=keys_stage, queries=queries_stage,
                          heads0=lambda g: heads_stage(g, 0), heads1=lambda g: heads_stage(g, 4),
                          residual=residual_stage, embed=embed_stage)

            def gather_segment(g, j):
                base = g * KSEL + j * LOOPS * SLOTS
                with act.Fori(0, LOOPS) as it:
                    for b in range(SLOTS // BATCH):
                        at = slice(b * BATCH, (b + 1) * BATCH)
                        act.wait_ge(dotted, it * SLOTS + (base + (b + 1) * BATCH))
                        nc.scalar.activation(act_a[:, at], a[:, at], ACT.Gelu_apprx_tanh).then_inc(gelued, 1)
                        act.wait_ge(weighted, it * (SLOTS // BATCH) + (base // BATCH + b + 1))
                        for s in range(b * BATCH, (b + 1) * BATCH):
                            act.wait_ge(slots_free, it * SLOTS + (base + s + 1))
                            nc.scalar.activation(diag[s][:], ident, ACT.Copy, scale=w[:, s:s + 1]
                                                 ).then_inc(diag_ready, 1)

            act.wait_ge(const_loaded, 16 * CONSTS)
            act.wait_ge(trig_shifted, 1)
            for stage, g in front(0):
                if stage in stages:
                    stages[stage](g)
                if stage == "pool":
                    nc.scalar.activation(cs[:, :, :, :], cs[:, :, :, :], ACT.Sin).then_inc(trig_done, 1)
            for g in range(PAIRS):
                for j in range(SEGMENTS):
                    for stage, gg in segment_stages(g, j):
                        if stage in stages:
                            stages[stage](gg)
                    gather_segment(g, j)
            for stage, g in back(PAIRS - 1):
                stages[stage](g)
            act.wait_ge(out_stored, 16 * NC)

        @block.vector
        def _(dve):
            steps = [0]

            def step(ins):
                ins.then_inc(dve_steps, 1)
                steps[0] += 1

            def settle():
                dve.wait_ge(dve_steps, steps[0])

            def reciprocal_rms(stage, g, i=0):
                n = norm_number(stage, g, i)
                dve.wait_ge(normed, n + 1)
                step(nc.vector.reciprocal(rstd[:, n:n + 1], rms[:, n:n + 1]))
                settle()
                return rstd[:, n:n + 1]

            def columns(at, n):
                return gc[:, at:at + n].unsqueeze(2).broadcast_to([P, n, P])

            def pool_stage(g):
                r = reciprocal_rms("pool", g)
                if g >= 2:
                    dve.wait_ge(t_filled, after("t_filled", "pool", g - 1))
                nc.vector.scalar_tensor_tensor(A[:, g % 2, :], X[:, g, :], r, mix_gain, ALU.mult, ALU.mult
                                               ).then_inc(mixed, 1)
                dve.wait_ge(weights_used, used("pool_w", g, 0))
                step(nc.vector.tensor_tensor(TU[:, :], M[:, :], pool_scale, ALU.mult))
                settle()
                nc.vector.tensor_tensor(X[:, g, :], X[:, g, :], TU[:, :], ALU.add).then_inc(x_ready, 1)

            def query_stage(g):
                r = reciprocal_rms("query", g)
                if g == NC:
                    dve.wait_ge(gain_loaded, 16)
                if g - 2 >= NC:
                    dve.wait_ge(out_stored, 16 * (g - 2 - NC + 1))
                nc.vector.scalar_tensor_tensor(HP[:, g % 2, :], X[:, g % NC, :], r, ffn_gain[:, :], ALU.mult, ALU.mult
                                               ).then_inc(hp_ready, 1)

            def top16(n, values, left, tops, places):
                for i in range(n):
                    step(nc.vector.max(tops(i)[:, 0:8], values(i)))
                settle()
                for i in range(n):
                    step(nc.vector.match_replace(left(i), tops(i)[:, 0:8], values(i), LOW))
                    step(nc.vector.max_index(places(i)[:, 0:8], tops(i)[:, 0:8], values(i)))
                settle()
                for i in range(n):
                    step(nc.vector.max(tops(i)[:, 8:16], left(i)))
                settle()
                for i in range(n):
                    step(nc.vector.max_index(places(i)[:, 8:16], tops(i)[:, 8:16], left(i)))
                settle()

            def score_stage(g):
                dve.wait_ge(m_copied, after("m_copied", "score", g))
                top16(2 * PH, lambda i: scores[:, i, :], lambda i: rest[:, i, :],
                      lambda i: top[:, i // 2, i % 2, :], lambda i: top_u[:, i // 2, i % 2, :])
                step(nc.vector.tensor_copy(top_i[:, :, :, :], top_u[:, :, :, :]))
                cand = SC[:, :].rearrange("p (h i j) -> p h i j", h=PH, i=TOPK)
                step(nc.vector.tensor_tensor(cand, top[:, :, 0, :].unsqueeze(3).broadcast_to([P, PH, TOPK, TOPK]),
                                             top[:, :, 1, :].unsqueeze(2).broadcast_to([P, PH, TOPK, TOPK]), ALU.add))
                settle()

            def pick_stage(g):
                n2 = TOPK * TOPK
                top16(PH, lambda i: SC[:, i * n2:(i + 1) * n2], lambda i: SD[:, i * n2:(i + 1) * n2],
                      lambda i: best[:, i, :], lambda i: pos_u[:, i, :])

            def select_stage(g):
                nc.vector.tensor_tensor(shifted[:, :, :], best[:, :, :], best[:, :, 0:1].broadcast_to([P, PH, TOPK]),
                                        ALU.subtract).then_inc(gate_shifted, 1)
                flat = pos_u[:, :, :].rearrange("p h k -> p (h k)")
                step(nc.vector.tensor_scalar(half_u[:, 0, :], flat, 4, None, ALU.logical_shift_right))
                step(nc.vector.tensor_scalar(half_u[:, 1, :], flat, TOPK - 1, None, ALU.bitwise_and))
                settle()
                step(nc.vector.tensor_copy(half_f[:, :, :], half_u[:, :, :]))
                settle()
                onehot = [SC, SD]
                for p in range(2):
                    step(nc.vector.tensor_tensor(
                        onehot[p][:, :].rearrange("p (n j) -> p n j", j=TOPK),
                        half_f[:, p, :].unsqueeze(2).broadcast_to([P, KSEL, TOPK]),
                        iota.unsqueeze(1).broadcast_to([P, KSEL, TOPK]), ALU.is_equal))
                settle()
                for p in range(2):
                    v = onehot[p][:, :].rearrange("p (h k j) -> p h k j", h=PH, k=TOPK)
                    step(nc.vector.tensor_tensor(
                        v, v, top_i[:, :, p, :].unsqueeze(2).broadcast_to([P, PH, TOPK, TOPK]), ALU.mult))
                settle()
                for p in range(2):
                    step(nc.vector.reduce_sum(sel[:, p, :], onehot[p][:, :].rearrange("p (n j) -> p n j", j=TOPK),
                                              axis=AX))
                settle()
                nc.vector.scalar_tensor_tensor(idx[:, g % 2, :], sel[:, 0, :], float(P), sel[:, 1, :],
                                               ALU.mult, ALU.add).then_inc(idx_ready, 1)
                dve.wait_ge(gate_exped, g + 1)
                step(nc.vector.reduce_sum(gsum[:, :], shifted[:, :, :], axis=AX))
                settle()
                step(nc.vector.reciprocal(grec[:, :], gsum[:, :]))
                settle()
                step(nc.vector.tensor_tensor(gate[:, g % 2, :].rearrange("p (h k) -> p h k", h=PH), shifted[:, :, :],
                                             grec[:, :].unsqueeze(2).broadcast_to([P, PH, TOPK]), ALU.mult))
                settle()

            def rope(dst, src, heads, c, tmp):
                def bc(i):
                    return cs[:, i, c, :].unsqueeze(1).broadcast_to([P, heads, HALF])
                s3 = src.rearrange("p (h d) -> p h d", h=heads)
                d3 = dst.rearrange("p (h d) -> p h d", h=heads)
                n = heads * HALF
                t3 = tmp[:, 0:n].rearrange("p (h d) -> p h d", h=heads)
                u3 = tmp[:, 256:256 + n].rearrange("p (h d) -> p h d", h=heads)
                lo, hi = slice(0, HALF), slice(HALF, ROPE)
                step(nc.vector.tensor_tensor(d3[:, :, lo], s3[:, :, lo], bc(0), ALU.mult))
                step(nc.vector.tensor_tensor(t3, s3[:, :, hi], bc(1), ALU.mult))
                step(nc.vector.tensor_tensor(d3[:, :, hi], s3[:, :, hi], bc(0), ALU.mult))
                step(nc.vector.tensor_tensor(u3, s3[:, :, lo], bc(1), ALU.mult))
                settle()
                step(nc.vector.tensor_tensor(d3[:, :, lo], d3[:, :, lo], t3, ALU.subtract))
                return nc.vector.tensor_tensor(d3[:, :, hi], d3[:, :, hi], u3, ALU.add)

            def latent_stage(g):
                c = g % NC
                r = reciprocal_rms("latent", g)
                nc.vector.tensor_scalar(A[:, 0, :], X[:, c, :], r, None, ALU.mult).then_inc(hat_ready, 1)
                dve.wait_ge(t_filled, before("t_filled", "latent", g) + 1)
                tv = T[:, :].rearrange(blocks, t=P)
                nc.vector.tensor_tensor(TU[:, :].rearrange(blocks, t=P), tv, columns(G_KV, DB), ALU.mult)
                nc.vector.tensor_tensor(TT[:, :, :], tv, columns(G_MIX1, DB), ALU.mult).then_inc(t_copied, 1)
                dve.wait_ge(weights_used, used("w_dkv", g, 1))
                if g == NC:
                    dve.wait_ge(trig_done, 1)
                step(rope(kpe, M[:, 512:512 + ROPE], 1, c, rtmp))
                r = reciprocal_rms("latent", g, 1)
                nc.vector.tensor_scalar(ckv, M[:, 0:KVR], r, None, ALU.mult).then_inc(m_copied, 1)
                dve.wait_ge(t_filled, after("t_filled", "latent", g))
                nc.vector.tensor_tensor(ckvT.rearrange(blocks, t=P), T[:, 0:KVR].rearrange(blocks, t=P),
                                        columns(G_CKV, KVR // P), ALU.mult)
                nc.vector.tensor_copy(KPE[:, c * P:(c + 1) * P], T[0:ROPE, KVR:KVR + P]).then_inc(t_copied, 1)

            def keys_stage(g):
                r = reciprocal_rms("keys", g)
                nc.vector.tensor_scalar(A[:, 1, 0:QR], M[:, 0:QR], r, None, ALU.mult).then_inc(m_copied, 1)

            def queries_stage(g):
                dve.wait_ge(t_filled, before("t_filled", "queries", g) + 1)
                n = QR // P
                nc.vector.tensor_tensor(TT[:, 0:n, :], T[:, 0:QR].rearrange(blocks, t=P), columns(G_Q, n), ALU.mult
                                        ).then_inc(t_copied, 1)
                dve.wait_ge(weights_used, used("w_uq_pe", g, 1))
                rope(qpe, M[:, 0:H * ROPE], H, g % NC, rtmp).then_inc(m_copied, 1)

            def heads_stage(g, first):
                c = g % NC
                width = (c + 1) * P

                def largest(h):
                    n = c * H + h
                    s = B[:, (h % 2) * 512:(h % 2) * 512 + width]
                    dve.wait_ge(att_scored, n + 1)
                    step(nc.vector.tensor_tensor(s[:, c * P:width], s[:, c * P:width], mask, ALU.add))
                    settle()
                    step(nc.vector.reduce_max(amax[:, n:n + 1], s, axis=AX))
                    settle()
                    nc.vector.tensor_scalar(nmax[:, n:n + 1], amax[:, n:n + 1], -SCALE, None, ALU.mult
                                            ).then_inc(att_maxed, 1)

                if first == 0:
                    largest(0)
                    largest(1)
                for h in range(first, first + 4):
                    n = c * H + h
                    dve.wait_ge(att_exped, n + 1)
                    step(nc.vector.reciprocal(arec[:, n:n + 1], asum[:, n:n + 1]))
                    settle()
                    nc.vector.tensor_scalar(prob[h % 2][:, 0:width], prob[h % 2][:, 0:width], arec[:, n:n + 1], None,
                                            ALU.mult).then_inc(att_normed, 1)
                    if h + 2 < H:
                        largest(h + 2)

            def project_stage(g):
                dve.wait_ge(weights_used, used("w_o", g, 3))
                nc.vector.tensor_tensor(X[:, g % NC, :], X[:, g % NC, :], M[:, :], ALU.add).then_inc(x_ready, 1)

            def residual_stage(g):
                dve.wait_ge(acc_done, g + 1)
                nc.vector.tensor_tensor(X[:, g % NC, :], X[:, g % NC, :], acc[:, :], ALU.add).then_inc(x_ready, 1)
                r = reciprocal_rms("residual", g)
                nc.vector.tensor_scalar(TU[:, :], X[:, g % NC, :], r, None, ALU.mult).then_inc(hat_ready, 1)
                dve.wait_ge(t_filled, after("t_filled", "residual", g))
                nc.vector.tensor_tensor(TT[:, :, :], T[:, :].rearrange(blocks, t=P), columns(G_PLE + (g // NC) * DB, DB),
                                        ALU.mult).then_inc(t_copied, 1)

            def embed_stage(g):
                dve.wait_ge(weights_used, used("ple_wp", g, 0))
                dve.wait_ge(m_copied, after("m_copied", "embed", g))
                nc.vector.tensor_tensor(TU[:, :], TU[:, :], B[:, :], ALU.mult).then_inc(s_copied, 1)
                dve.wait_ge(s_copied, after("s_copied", "embed", g))
                nc.vector.tensor_tensor(X[:, g % NC, :], X[:, g % NC, :], TU[:, :], ALU.add).then_inc(x_ready, 1)
                if g >= NC:
                    r = reciprocal_rms("embed", g)
                    nc.vector.scalar_tensor_tensor(HP[:, g % 2, :], X[:, g % NC, :], r, final_gain[:, :],
                                                   ALU.mult, ALU.mult).then_inc(out_ready, 1)

            stages = dict(pool=pool_stage, query=query_stage, score=score_stage, pick=pick_stage,
                          select=select_stage, latent=latent_stage, keys=keys_stage, queries=queries_stage,
                          heads0=lambda g: heads_stage(g, 0), heads1=lambda g: heads_stage(g, 4),
                          project=project_stage, residual=residual_stage, embed=embed_stage)

            def gather_segment(g, j):
                base = g * KSEL + j * LOOPS * SLOTS
                with dve.Fori(0, LOOPS) as it:
                    for b in range(SLOTS // BATCH):
                        for s in range(b * BATCH, (b + 1) * BATCH):
                            dve.wait_ge(rows_loaded[s], it * 16 + 16 * (base // SLOTS + 1))
                            nc.vector.tensor_tensor_reduce(
                                out=slot[s][:, 0:D], in0=slot[s][:, 0:D], in1=HP[:, g % 2, :], scale=1.0, scalar=0.0,
                                op0=ALU.mult, op1=ALU.add, accum_out=a[:, s:s + 1]).then_inc(dotted, 1)
                        at = slice(b * BATCH, (b + 1) * BATCH)
                        dve.wait_ge(gelued, it * (SLOTS // BATCH) + (base // BATCH + b + 1))
                        nc.vector.tensor_tensor(
                            w[:, at], act_a[:, at],
                            gate[:, g % 2, bass.ds(it * SLOTS + (j * LOOPS * SLOTS + b * BATCH), BATCH)], ALU.mult
                        ).then_inc(weighted, 1)

            nc.vector.memset(zeros[:], 0.0).then_inc(zeroed, 1)
            dve.wait_ge(const_loaded, 16 * CONSTS)
            step(nc.vector.tensor_copy(pos_f[:], pos_i[:]))
            settle()
            angle, turns = SC[:, 0:NC * HALF], SC[:, 512:512 + NC * HALF]
            magic = float(np.float32(1.5 * 2 ** 23))
            part1 = 6.28125
            part2 = float(np.float32(np.float32(0.0019350051879882812)))
            part3 = float(np.float32(2 * np.pi - part1 - part2))
            for c in range(NC):
                step(nc.vector.tensor_scalar(angle[:, c * HALF:(c + 1) * HALF], inv, pos_f[:, c:c + 1], None, ALU.mult))
            settle()
            for i, ahead in ((0, 0.25), (1, 0.0)):
                dst = cs[:, i, :, :].rearrange("p c d -> p (c d)")
                step(nc.vector.tensor_scalar(turns, angle, float(1 / (2 * np.pi)), ahead, ALU.mult, ALU.add))
                settle()
                step(nc.vector.tensor_scalar(turns, turns, magic, None, ALU.add))
                settle()
                step(nc.vector.tensor_scalar(turns, turns, -magic, None, ALU.add))
                settle()
                step(nc.vector.scalar_tensor_tensor(dst, turns, -part1, angle, ALU.mult, ALU.add))
                settle()
                step(nc.vector.scalar_tensor_tensor(dst, turns, -part2, dst, ALU.mult, ALU.add))
                settle()
                step(nc.vector.scalar_tensor_tensor(dst, turns, -part3, dst, ALU.mult, ALU.add))
                settle()
                step(nc.vector.tensor_scalar(dst, dst, float(np.pi / 2) if ahead else 0.0, float(np.float32(3.1415925)),
                                             ALU.add, ALU.min))
                settle()
                last = nc.vector.tensor_scalar(dst, dst, -float(np.float32(3.1415925)), None, ALU.max)
                if i == 0:
                    step(last)
                    settle()
            last.then_inc(trig_shifted, 1)

            for stage, g in front(0):
                stages[stage](g)
            for g in range(PAIRS):
                for j in range(SEGMENTS):
                    for stage, gg in segment_stages(g, j):
                        stages[stage](gg)
                    gather_segment(g, j)
            for stage, g in back(PAIRS - 1):
                stages[stage](g)


def shape_constants():
    t = np.arange(P)
    c = np.zeros((P, C_WIDTH), np.float32)
    c[:, C_IDENT:C_IDENT + P] = np.eye(P)
    c[:, C_MASK:C_MASK + P] = np.where(t[None, :] <= t[:, None], 0.0, -1.0e30)
    c[:, C_IOTA:C_IOTA + TOPK] = np.arange(TOPK)
    c[:, C_INV:C_INV + HALF] = np.float32(10000.0) ** (-np.arange(0, ROPE, 2, dtype=np.float32) / ROPE)
    c[:, C_EPS] = EPS
    pools = np.zeros((P, 3, len(WINDOWS), P), np.float32)
    for n, w in enumerate(WINDOWS):
        d = t[None, :] - t[:, None]
        inside = (d >= 0) & (d < w)
        pools[:, 0, n] = inside / np.minimum(t + 1, w)[None, :] - np.eye(P)
        pools[:, 1, n] = inside / w - np.eye(P)
        pools[:, 2, n] = (d + P < w) / w
    return c, pools.reshape(P, -1)


def by_columns(w, cols):
    k, n = w.shape
    return np.ascontiguousarray(w.reshape(k // P, P, n // cols, cols).transpose(2, 1, 0, 3).reshape(n // cols, P, -1))


def kernel(x, p, positions, mix_norm, ffn_norm, pool_w, pool_scale, kv_in_norm, w_dkv, kv_norm, w_ukv,
           w_dq, q_norm, w_uq, w_o, peer_wq, peer_keys, peer_u, peer_v, ple_norm, ple_wg, ple_wp, final_norm):
    import concourse.bacc as bacc
    from concourse.bass_utils import run_bass_kernel_spmd as run

    (x, p, positions, mix_norm, ffn_norm, pool_w, pool_scale, kv_in_norm, w_dkv, kv_norm, w_ukv, w_dq, q_norm, w_uq,
     w_o, peer_wq, peer_keys, peer_u, peer_v, ple_norm, ple_wg, ple_wp, final_norm) = (
        np.asarray(v) for v in (
            x, p, positions, mix_norm, ffn_norm, pool_w, pool_scale, kv_in_norm, w_dkv, kv_norm, w_ukv, w_dq, q_norm,
            w_uq, w_o, peer_wq, peer_keys, peer_u, peer_v, ple_norm, ple_wg, ple_wp, final_norm))

    consts, pools = shape_constants()
    arrays = {
        "consts": consts,
        "pools": pools,
        "gcols": np.concatenate([v.reshape(-1, P).T for v in (kv_in_norm, mix_norm[1], ple_norm[0], ple_norm[1],
                                                              kv_norm, q_norm[0])], axis=1),
        "gains": np.stack([mix_norm[0], pool_scale[0], ffn_norm[0], ffn_norm[1], final_norm]),
        "positions": positions.reshape(NC, P).T,
        "x": x.reshape(S, D),
        "pT": p.reshape(DEPTH, S, PLE // P, P).transpose(0, 3, 2, 1),
    }
    for l in range(DEPTH):
        arrays[f"uv{l}"] = np.concatenate([peer_u[l], peer_v[l]], axis=1)
    heads_kv = w_ukv.reshape(KVR, H, NOPE + VH)
    heads_q = w_uq[0].reshape(QR, H, NOPE + ROPE)
    per_layer = {
        ("pool_w", 0): pool_w[0].reshape(len(WINDOWS), 2, P, GW).transpose(2, 0, 1, 3).reshape(1, P, -1),
        ("w_ukv_k", 1): by_columns(heads_kv[:, :, :NOPE].reshape(KVR, -1), H * NOPE),
        ("w_ukv_v", 1): by_columns(heads_kv[:, :, NOPE:].reshape(KVR, -1), H * VH),
        ("w_dq", 1): by_columns(w_dq[0], 256),
        ("w_uq_nope", 1): by_columns(heads_q[:, :, :NOPE].reshape(QR, -1), 256),
        ("w_uq_pe", 1): by_columns(heads_q[:, :, NOPE:].reshape(QR, -1), 256),
        ("w_o", 1): by_columns(w_o[0], 256),
    }
    for l in range(DEPTH):
        per_layer["wq", l] = by_columns(peer_wq[l], 256)
        per_layer["keys", l] = peer_keys[l].reshape(2 * PH, P, P).transpose(2, 0, 1).reshape(1, P, -1)
        per_layer["ple_wg", l] = by_columns(ple_wg[l], 256)
        per_layer["ple_wp", l] = by_columns(ple_wp[l], D)
    for (name, l), v in per_layer.items():
        arrays[f"{name}_{l}"] = v
    arrays["w_dkv_a"] = by_columns(w_dkv[:, :KVR], KVR)
    arrays["w_dkv_b"] = by_columns(w_dkv[:, KVR:], ROPE)
    arrays = {n: np.ascontiguousarray(v) for n, v in arrays.items()}

    nc = bacc.Bacc("TRN2", target_bir_lowering=False, num_devices=1)
    ap = {n: nc.dram_tensor(f"in_{n}", v.shape, mybir.dt.from_np(v.dtype), kind="ExternalInput").ap()
          for n, v in arrays.items()}
    out = nc.dram_tensor("out", (S, D), F32, kind="ExternalOutput").ap()
    weights = {(name, l): [ap[f"{name}_{l}"][i] for i in range(v.shape[0])] for (name, l), v in per_layer.items()}
    weights["w_dkv", 1] = [ap["w_dkv_a"][0], ap["w_dkv_b"][0]]
    trunk(nc, ap["consts"], ap["pools"], ap["gcols"], ap["gains"], ap["positions"], ap["x"], ap["pT"],
          [ap["uv0"], ap["uv1"]], weights, out)
    r = run(nc, [{f"in_{n}": v for n, v in arrays.items()}], core_ids=[0])
    return r.results[0]["out"].reshape(1, S, D)
```

```python
import numpy as np
import concourse.bass as bass
from concourse import mybir
from contextlib import ExitStack

F32 = mybir.dt.float32
BF16 = mybir.dt.bfloat16
I32 = mybir.dt.int32
U32 = mybir.dt.uint32
ALU = mybir.AluOpType
ACT = mybir.ActivationFunctionType
AX = mybir.AxisListType.X

P = 128
S, D, DEPTH = 512, 1024, 2
NC = S // P
DB = D // P
PAIRS = DEPTH * NC
WINDOWS = (2, 4, 8, 16)
GW = D // len(WINDOWS)
H, NOPE, ROPE, VH = 8, 128, 64, 128
HEAD_PAIRS = H // 2
HALF = ROPE // 2
QR, KVR = 768, 256
SCALE = 1.0 / float(np.sqrt(NOPE + ROPE))
PH, TOPK = 8, 16
KSEL = PH * TOPK
NEXP = P * P
PLE = 256
EPS = 1e-6
LOW = -3.0e38

RING = 2
PIECE = 2048
GROUP = 2
SLOTS = 8
BATCH = 4
BODIES = KSEL // SLOTS
DVE_SLOTS = (3, 7)
PE_SLOTS = tuple(s for s in range(SLOTS) if s not in DVE_SLOTS)
NPE, NDVE = len(PE_SLOTS), len(DVE_SLOTS)
HPB = 3

C_IDENT, C_MASK, C_IOTA, C_INV, C_EPS = 0, P, 2 * P, 2 * P + TOPK, 2 * P + TOPK + HALF
C_WIDTH = C_EPS + 1
G_KV, G_MIX1, G_PLE, G_CKV, G_Q = 0, DB, 2 * DB, 4 * DB, 4 * DB + KVR // P
G_WIDTH = G_Q + QR // P


def stages_of(names, g0, n):
    return [(name, g0, n) for name in names]


def rank(g):
    return stages_of(["pick", "select"], g, 1)


def ffn(g0, n):
    return stages_of(["fnorm", "asks"], g0, n) + rank(g0)


def embed(g0, n):
    return stages_of(["enorm", "gates", "add"], g0, n)


def residual(g):
    return stages_of(["residual"], g, 1)


def mix_a(g0):
    return stages_of(["latent", "keys", "dq", "uq", "uqp"], g0, 2) + stages_of(["heads"], g0, 1)


def mix_b(g0):
    return stages_of(["heads"], g0 + 1, 1) + stages_of(["wo"], g0, 2)


START = stages_of(["pool"], 0, 1) + ffn(0, 1)
STEPS = [
    stages_of(["pool"], 1, 1) + ffn(1, 1),
    residual(0) + stages_of(["pool"], 2, 2) + ffn(2, 2),
    residual(1) + rank(3) + embed(0, 2) + mix_a(4),
    residual(2) + mix_b(4) + ffn(4, 2),
    residual(3) + rank(5) + embed(2, 2) + mix_a(6),
    residual(4) + mix_b(6) + ffn(6, 2),
    residual(5) + rank(7) + embed(4, 2),
    residual(6) + embed(6, 1),
]
END = residual(7) + embed(7, 1)
SCHEDULE = START + [st for step in STEPS for st in step] + END

USES = {"pool": [("pool_w", [0])], "latent": [("w_dkv", [0, 1])],
        "keys": [("w_ukv_k", [0]), ("w_ukv_v", [0])], "dq": [("w_dq", [0, 1, 2])],
        "uq": [("w_uq_nope", [0, 1, 2, 3])], "uqp": [("w_uq_pe", [0, 1])], "wo": [("w_o", [0, 1, 2, 3])],
        "asks": [("wq", list(range(PH)))], "gates": [("ple_wg", [0, 1, 2, 3])], "add": [("ple_wp", [0])]}

PARTS = {
    "pool": lambda n: [2] + [4, 5] * n + [2],
    "fnorm": lambda n: [2] + [3] * n + [1],
    "asks": lambda n: [5 * n] + [6 * n] * (PH - 1) + [3 * n] * 2,
    "pick": lambda n: [7, 7],
    "select": lambda n: [8, 8, 2],
    "residual": lambda n: [2, 0],
    "enorm": lambda n: [2] + [3] * n + [1],
    "gates": lambda n: [5 * n] * 4 + [2],
    "add": lambda n: [5 * n, 4, 1, 1],
    "latent": lambda n: [2, 4, 5, 10, 4, 3, 2],
    "keys": lambda n: [9, 9, 2],
    "dq": lambda n: [9, 9, 9, 2, 4, 4, 2],
    "uq": lambda n: [7, 7, 7, 7, 1],
    "uqp": lambda n: [7, 7, 5, 3, 3, 1],
    "heads": lambda n: [3, 5, 8, 8, 6, 5, 3, 1],
    "wo": lambda n: [9, 9, 9, 9, 2],
}


def incs(stage, g0, n):
    second = 1 if n == 2 else 0
    return {
        "pool": dict(normed=n, t_filled=n, t_copied=n, x_ready=n, pooled=n - 1),
        "fnorm": dict(normed=n, hp_ready=n, t_filled=n, t_copied=n),
        "select": dict(idx_ready=1),
        "latent": dict(normed=2 * n, hat_ready=n, t_filled=n + 1, t_copied=n + 1, m_copied=1, b_copied=1),
        "keys": dict(m_copied=2, b_copied=2),
        "dq": dict(normed=n, m_copied=1, b_copied=1, t_filled=n, t_copied=n),
        "uq": dict(m_copied=1, b_copied=1),
        "uqp": dict(m_copied=1, b_copied=1, t_filled=n, t_copied=n),
        "heads": dict(m_copied=2),
        "wo": dict(x_ready=n),
        "residual": dict(x_ready=1),
        "enorm": dict(normed=n, hat_ready=n, t_filled=n, t_copied=n),
        "gates": dict(m_copied=1, b_copied=second),
        "add": dict(m_copied=1, b_copied=second, x_ready=n, normed=n if g0 >= NC else 0),
        "asks": dict(b_copied=PH // 2, m_copied=PH // 2, t_filled=PH, t_copied=PH),
    }.get(stage, {})


def totals():
    count, at = {}, {}
    for st in SCHEDULE:
        at[st[:2]] = dict(count)
        for name, n in incs(*st).items():
            count[name] = count.get(name, 0) + n
    return at, count


AT, TOTAL = totals()
FFN_GROUPS = [g0 for s, g0, n in SCHEDULE if s == "fnorm"]
EMBED_GROUPS = [g0 for s, g0, n in SCHEDULE if s == "enorm"]
PLACE = {g0 + i: i for s, g0, n in SCHEDULE if s == "fnorm" for i in range(n)}


def before(name, stage, g0):
    return AT[stage, g0].get(name, 0)


PIECES = {}
for _stage, _g, _n in SCHEDULE:
    for _w, _is in USES.get(_stage, []):
        for _i in _is:
            PIECES[_w, _g, _i] = len(PIECES)


def placed_parts(g):
    placed, done = [[] for _ in range(BODIES)], 0
    total = sum(sum(PARTS[st[0]](st[2])) for st in STEPS[g])
    for st in STEPS[g]:
        for part, share in enumerate(PARTS[st[0]](st[2])):
            placed[done * (BODIES - 1) // total].append((st, part))
            done += share
    return placed


def run_between(stages, gather_bodies, open_pair=None, close_pair=None):
    running = {}

    def run_part(st, part):
        stage, g0, n = st
        if stage not in stages:
            return
        if part == 0:
            running[st] = stages[stage](g0, n)
        ended = next(running[st], "ended")
        assert part < len(PARTS[stage](n)) - 1 or ended == "ended", (stage, part)

    def run_all(sts):
        for st in sts:
            for part in range(len(PARTS[st[0]](st[2]))):
                run_part(st, part)

    run_all(START)
    for g in range(PAIRS):
        if open_pair:
            open_pair(g)
        placed = placed_parts(g)
        starts = [j for j in range(BODIES) if placed[j] or j == 0]
        for j, end in zip(starts, starts[1:] + [BODIES]):
            for st, part in placed[j]:
                run_part(st, part)
            gather_bodies(g, j, end - j)
        if close_pair:
            close_pair(g)
    run_all(END)


def run_bodies(engine, count, body):
    if count == 1:
        body(0)
    else:
        with engine.Fori(0, count) as it:
            body(it)


def trunk(nc, consts, pools, gcols, gains, positions, x, pT, uv, weights, keys, out):
    ctx = ExitStack()
    with ctx:
        def sb(name, shape, dt=F32):
            return ctx.enter_context(nc.sbuf_tensor(name, shape, dt))

        def sem(name):
            return ctx.enter_context(nc.semaphore(name))

        W2 = GROUP * P
        X = sb("X", [P, NC, D])
        KV = sb("KV", [P, 2 * NC * D])
        KT = KV[:, 0:NC * D].rearrange("p (h s) -> p h s", h=H)
        V = KV[:, NC * D:2 * NC * D].rearrange("p (c d) -> p c d", c=NC)
        poolm = KV[:, 0:12 * P].rearrange("p (k w t) -> p k w t", k=3, w=4)
        mix_gain = KV[:, 12 * P:12 * P + D]
        pool_scale = KV[:, 12 * P + D:12 * P + 2 * D]
        hpool = KV[:, 12 * P + 2 * D:12 * P + 4 * D].rearrange("p (i d) -> p i d", i=2)
        KPE = sb("KPE", [ROPE, S])
        cs = sb("cs", [P, 2, NC, HALF])
        cst = sb("cst", [P, C_WIDTH])
        gc = sb("gc", [P, G_WIDTH])
        gain = sb("gain", [P, D])
        HP = sb("HP", [P, HPB, D])
        A = sb("A", [P, 2, D])
        TT = sb("TT", [P, DB, W2])
        TU = sb("TU", [P, DB, W2])
        SC = sb("SC", [P, PIECE])
        SD = sb("SD", [P, PIECE])
        sq_out = sb("sq_out", [P, D], BF16)
        ring = [sb(f"w{i}", [P, PIECE]) for i in range(RING)]
        pt = sb("pt", [P, PLE // P, W2])
        ss = sb("ss", [P, TOTAL["normed"]])
        rms = sb("rms", [P, TOTAL["normed"]])
        rstd = sb("rstd", [P, TOTAL["normed"]])
        slot = [sb(f"slot{i}", [P, 2 * D]) for i in range(SLOTS)]
        diag = {s: sb(f"diag{s}", [P, P]) for s in PE_SLOTS}
        a = sb("a", [P, SLOTS])
        act_a = sb("act_a", [P, SLOTS])
        w = sb("w", [P, SLOTS])
        idx = sb("idx", [P, HPB, KSEL], I32)
        gate = sb("gate", [P, HPB, KSEL])
        top = sb("top", [P, GROUP, PH, 2, TOPK])
        top_u = sb("top_u", [P, GROUP, PH, 2, TOPK], U32)
        top_i = sb("top_i", [P, PH, 2, TOPK])
        best = sb("best", [P, PH, TOPK])
        pos_u = sb("pos_u", [P, PH, TOPK], U32)
        half_f = sb("half_f", [P, 2, KSEL])
        shifted = sb("shifted", [P, PH, TOPK])
        gsum = sb("gsum", [P, PH])
        grec = sb("grec", [P, PH])
        amax = sb("amax", [P, NC * H])
        nmax = sb("nmax", [P, NC * H])
        asum = sb("asum", [P, NC * H])
        arec = sb("arec", [P, NC * H])
        pos_i = sb("pos_i", [P, NC], I32)
        pos_f = sb("pos_f", [P, NC])
        zeros = sb("zeros", [P, P])

        ident = cst[:, C_IDENT:C_IDENT + P]
        mask = cst[:, C_MASK:C_MASK + P]
        iota = cst[:, C_IOTA:C_IOTA + TOPK]
        inv = cst[:, C_INV:C_INV + HALF]
        eps = cst[:, C_EPS:C_EPS + 1]

        def ps(name, width):
            return ctx.enter_context(nc.psum_tensor(name, [P, width], F32))

        acc = ps("acc", D)
        M = ps("M", D)
        T = ps("T", D)
        B = ps("B", D)
        MB = (M, B)
        blocks = "p (b t) -> p b t"

        asked = A[:, :, :].rearrange("p a (q t) -> p a q t", q=4)[:, :, 0:2, :]
        ckv = [SD[:, 320 * i:320 * i + KVR] for i in range(2)]
        kpe = [SD[:, 320 * i + KVR:320 * (i + 1)] for i in range(2)]
        ckvT = SD[:, 640:640 + 2 * W2].rearrange(blocks, b=2)
        qpe = [SD[:, 512 * i:512 * (i + 1)] for i in range(2)]
        rtmp = SD[:, 1536:2048]
        QT = TU
        QPT = A[0:ROPE, :, :].rearrange("p a (b t) -> p (a b) t", t=W2)
        keysT = TU[:, :, :].rearrange("p k (a t) -> p (k a) t", t=P)
        prob = SC[:, :].rearrange("p (k e s) -> p k e s", k=2, e=2)
        probT = SD[:, 0:D].rearrange("p (e s) -> p e s", e=2)
        adiag = SD[:, D:D + 2 * P].rearrange("p (e t) -> p e t", e=2)
        half_u = SC[:, 0:2 * KSEL].bitcast(U32).rearrange("p (i k) -> p i k", i=2)
        outs = [SC[:, 0:D], SC[:, D:2 * D], SD[:, 0:D], SD[:, D:2 * D]]

        const_loaded = sem("const_loaded")
        x_loaded = [sem(f"x_loaded{c}") for c in range(NC)]
        w_loaded = [sem(f"w_loaded{i}") for i in range(RING)]
        keys_loaded = sem("keys_loaded")
        pt_loaded = sem("pt_loaded")
        gain_loaded = sem("gain_loaded")
        weights_used = sem("weights_used")
        normed = sem("normed")
        hat_ready, hp_ready, x_ready = sem("hat_ready"), sem("hp_ready"), sem("x_ready")
        t_filled = sem("t_filled")
        t_copied, m_copied, b_copied = sem("t_copied"), sem("m_copied"), sem("b_copied")
        squared, mixed, pooled = sem("squared"), sem("mixed"), sem("pooled")
        att_scored, att_maxed, att_exped = sem("att_scored"), sem("att_maxed"), sem("att_exped")
        att_normed, att_turned, att_copied, att_out = (sem("att_normed"), sem("att_turned"),
                                                       sem("att_copied"), sem("att_out"))
        gate_shifted, gate_exped = sem("gate_shifted"), sem("gate_exped")
        idx_ready = sem("idx_ready")
        rows_loaded = [sem(f"rows_loaded{i}") for i in range(SLOTS)]
        dotted, gelued, weighted, diag_ready = sem("dotted"), sem("gelued"), sem("weighted"), sem("diag_ready")
        slots_free = sem("slots_free")
        v_added = sem("v_added")
        acc_done = sem("acc_done")
        out_ready, out_stored = sem("out_ready"), sem("out_stored")
        dve_steps = sem("dve_steps")
        trig_shifted, trig_done = sem("trig_shifted"), sem("trig_done")
        zeroed = sem("zeroed")
        copied = (m_copied, b_copied)

        def used(name, g0, i):
            return PIECES[name, g0, i] + 1

        def norm_number(stage, g0, i=0):
            return before("normed", stage, g0) + i

        CONSTS = 7
        block = ctx.enter_context(nc.Block())

        @block.sync
        def _(sp):
            sp.dma_start(X[:, 0, :], x[0:P, :]).then_inc(x_loaded[0], 16)
            sp.dma_start(cst[:], consts).then_inc(const_loaded, 16)
            sp.dma_start(mix_gain, gains[0:1, :].broadcast_to([P, D])).then_inc(const_loaded, 16)
            sp.dma_start(KV[:, 0:12 * P], pools).then_inc(const_loaded, 16)
            sp.dma_start(pool_scale, gains[1:2, :].broadcast_to([P, D])).then_inc(const_loaded, 16)
            sp.dma_start(gain[:], gains[2:3, :].broadcast_to([P, D])).then_inc(const_loaded, 16)
            sp.dma_start(gc[:], gcols).then_inc(const_loaded, 16)
            sp.dma_start(pos_i[:], positions).then_inc(const_loaded, 16)
            groups = 0
            for (name, g0, i), n in PIECES.items():
                size = {st[:2]: st[2] for st in SCHEDULE}
                if name == "ple_wp":
                    width, c = size["add", g0] * P, g0 % NC
                    if groups:
                        sp.wait_ge(weights_used, last_wp)
                    sp.dma_start(pt[:, :, 0:width], pT[g0 // NC, :, :, c * P:c * P + width]).then_inc(pt_loaded, 16)
                    groups, last_wp = groups + 1, n + 1
                if n >= RING:
                    sp.wait_ge(weights_used, n - RING + 1)
                src = weights[name, g0 // NC][i]
                sp.dma_start(ring[n % RING][:, 0:src.shape[1]], src).then_inc(w_loaded[n % RING], 16)
                if name == "wq" and i == 1:
                    sp.wait_ge(x_ready, before("x_ready", "fnorm", g0))
                    sp.dma_start(TU[:, :, :], keys[g0 // NC]).then_inc(keys_loaded, 16)
                    if g0 == 0:
                        for c in range(1, NC):
                            sp.dma_start(X[:, c, :], x[c * P:(c + 1) * P, :]).then_inc(x_loaded[c], 16)
                if (name, i) == ("wq", 7) and g0 in (NC - 2, PAIRS - 2):
                    sp.wait_ge(hp_ready, g0 + 2)
                    sp.dma_start(gain[:], gains[3 + g0 // NC:4 + g0 // NC, :].broadcast_to([P, D])
                                 ).then_inc(gain_loaded, 16)

        @block.gpsimd
        def _(pool):
            for g in range(PAIRS):
                pool.wait_ge(idx_ready, g + 1)
                for k in range(KSEL):
                    body, s = (g * KSEL + k) // SLOTS, k % SLOTS
                    if s in DVE_SLOTS:
                        pool.wait_ge(v_added, body * NDVE + DVE_SLOTS.index(s) + 1)
                    else:
                        pool.wait_ge(slots_free, body * NPE + PE_SLOTS.index(s) + 1)
                    nc.gpsimd.indirect_dma_start(
                        out=slot[s][:], out_offset=None, in_=uv[g // NC],
                        in_offset=bass.IndirectOffsetOnAxis(ap=idx[:, g % HPB, k:k + 1], axis=0),
                    ).then_inc(rows_loaded[s], 16)

        @block.tensor
        def _(pe):
            def piece(name, g0, i):
                n = PIECES[name, g0, i]
                pe.wait_ge(w_loaded[n % RING], 16 * (n // RING + 1))
                return ring[n % RING]

            def transposes(src, n, width=P, at=0):
                for b in range(n):
                    last = nc.tensor.transpose(T[0:width, at + b * P:at + (b + 1) * P],
                                               src[:, b * width:(b + 1) * width], ident)
                return last

            def product(dst, lhsT, i, wp, kb, cols):
                for k in range(kb):
                    last = nc.tensor.matmul(dst, lhsT[:, k, i * P:(i + 1) * P], wp[:, k * cols:(k + 1) * cols],
                                            start=(k == 0), stop=(k == kb - 1))
                return last

            def products(g0, n, name, pieces, lhsT, kb, cols, at=lambda i: i * 256):
                for i in pieces:
                    wp = piece(name, g0, i)
                    for ch in range(n):
                        last = product(MB[ch][:, at(i):at(i) + cols], lhsT, ch, wp, kb, cols)
                    last.then_inc(weights_used, 1)

            def wait_mb(stage, g0, n=2):
                for ch, name in list(enumerate(("m_copied", "b_copied")))[:n]:
                    if before(name, stage, g0):
                        pe.wait_ge(copied[ch], before(name, stage, g0))

            def pool_stage(g0, n):
                for i in range(n):
                    yield
                    g = g0 + i
                    pe.wait_ge(mixed, g + 1)
                    if g:
                        pe.wait_ge(t_copied, before("t_copied", "pool", g0) + i)
                    for b in range(DB):
                        wnd = b // 2
                        dst = T[:, b * P:(b + 1) * P]
                        if g:
                            nc.tensor.matmul(dst, hpool[:, (g - 1) % 2, b * P:(b + 1) * P], poolm[:, 2, wnd, :],
                                             start=True, stop=False)
                        last = nc.tensor.matmul(dst, hpool[:, g % 2, b * P:(b + 1) * P],
                                                poolm[:, 1 if g else 0, wnd, :], start=(g == 0), stop=True)
                    last.then_inc(t_filled, 1)
                    yield
                    pe.wait_ge(t_copied, before("t_copied", "pool", g0) + i + 1)
                    if i:
                        pe.wait_ge(x_ready, before("x_ready", "pool", g0) + i)
                    else:
                        wait_mb("pool", g0, 1)
                        wp = piece("pool_w", g0, 0)
                    for wnd in range(len(WINDOWS)):
                        for k in range(2):
                            last = nc.tensor.matmul(M[:, wnd * GW:(wnd + 1) * GW], TU[:, 2 * wnd + k, 0:P],
                                                    wp[:, (2 * wnd + k) * GW:(2 * wnd + k + 1) * GW],
                                                    start=(k == 0), stop=(k == 1))
                    last.then_inc(pooled if i < n - 1 else weights_used, 1)

            def fnorm_stage(g0, n):
                for i in range(n):
                    yield
                    pe.wait_ge(hp_ready, g0 + i + 1)
                    pe.wait_ge(t_copied, before("t_copied", "fnorm", g0) + i)
                    transposes(HP[:, (g0 + i) % HPB, :], DB).then_inc(t_filled, 1)

            def asks_stage(g0, n):
                width = n * P

                def queries(p):
                    dst, name = ((B, "b_copied"), (M, "m_copied"))[p % 2]
                    if before(name, "asks", g0) + p // 2:
                        pe.wait_ge((b_copied, m_copied)[p % 2], before(name, "asks", g0) + p // 2)
                    if p == 0:
                        pe.wait_ge(t_copied, before("t_copied", "asks", g0))
                    wp = piece("wq", g0, p)
                    for e in range(2):
                        for k in range(DB):
                            last = nc.tensor.matmul(dst[:, e * 512:e * 512 + width],
                                                    wp[:, k * 256 + e * P:k * 256 + (e + 1) * P],
                                                    TT[:, k, 0:width], start=(k == 0), stop=(k == DB - 1))
                    last.then_inc(weights_used, 1)

                def scores(p):
                    if p == 0:
                        pe.wait_ge(keys_loaded, 16 * (FFN_GROUPS.index(g0) + 1))
                    name = ("b_copied", "m_copied")[p % 2]
                    pe.wait_ge((b_copied, m_copied)[p % 2], before(name, "asks", g0) + p // 2 + 1)
                    if p >= 2:
                        pe.wait_ge(t_copied, before("t_copied", "asks", g0) + p - 1)
                    for i in range(n):
                        for e in range(2):
                            at = (p % 2) * 512 + (2 * i + e) * P
                            last = nc.tensor.matmul(T[:, at:at + P], asked[:, p % 2, e, i * P:(i + 1) * P],
                                                    keysT[:, 2 * p + e, :], start=True, stop=True)
                    last.then_inc(t_filled, 1)

                for p in range(PH):
                    queries(p)
                    if p:
                        scores(p - 1)
                    yield
                scores(PH - 1)

            def latent_stage(g0, n):
                t0 = before("t_copied", "latent", g0)
                for i in range(n):
                    yield
                    pe.wait_ge(hat_ready, before("hat_ready", "latent", g0) + i + 1)
                    pe.wait_ge(t_copied, t0 + i)
                    transposes(A[:, i, :], DB).then_inc(t_filled, 1)
                yield
                pe.wait_ge(t_copied, t0 + n)
                wait_mb("latent", g0)
                products(g0, n, "w_dkv", [0], TU, DB, KVR, lambda i: 0)
                products(g0, n, "w_dkv", [1], TU, DB, ROPE, lambda i: 512)
                yield
                yield
                for i in range(n):
                    pe.wait_ge(copied[i], before(("m_copied", "b_copied")[i], "latent", g0) + 1)
                    transposes(ckv[i], 2, at=512 * i)
                    last = nc.tensor.transpose(T[0:ROPE, 512 * i + KVR:512 * i + KVR + P], kpe[i], ident)
                last.then_inc(t_filled, 1)

            def keys_stage(g0, n):
                pe.wait_ge(t_copied, before("t_copied", "keys", g0))
                wait_mb("keys", g0)
                wp = piece("w_ukv_k", g0, 0)
                for h in range(H):
                    for k in range(2):
                        last = nc.tensor.matmul(MB[h // 4][:, (h % 4) * W2:(h % 4 + 1) * W2],
                                                wp[:, k * 1024 + h * P:k * 1024 + (h + 1) * P],
                                                ckvT[:, k, :], start=(k == 0), stop=(k == 1))
                last.then_inc(weights_used, 1)
                yield
                wp = piece("w_ukv_v", g0, 0)
                for i in range(n):
                    pe.wait_ge(copied[i], before(("m_copied", "b_copied")[i], "keys", g0) + 1)
                    for half in range(2):
                        last = product(MB[i][:, half * 512:half * 512 + 512], ckvT, i,
                                       wp[:, half * 1024:half * 1024 + 1024], 2, 512)
                last.then_inc(weights_used, 1)

            def dq_stage(g0, n):
                wait_mb("dq", g0)
                for i in range(3):
                    products(g0, n, "w_dq", [i], TT, DB, 256)
                    yield
                for i in range(n):
                    yield
                    pe.wait_ge(copied[i], before(("m_copied", "b_copied")[i], "dq", g0) + 1)
                    pe.wait_ge(t_copied, before("t_copied", "dq", g0) + i)
                    transposes(A[:, i, :], QR // P).then_inc(t_filled, 1)

            def uq_stage(g0, n):
                pe.wait_ge(t_copied, before("t_copied", "uq", g0))
                wait_mb("uq", g0)
                for q in range(4):
                    wp = piece("w_uq_nope", g0, q)
                    for e in range(2):
                        at = (2 * (q % 2) + e) * W2
                        for k in range(QR // P):
                            last = nc.tensor.matmul(MB[q // 2][:, at:at + W2],
                                                    wp[:, k * 256 + e * P:k * 256 + (e + 1) * P], TT[:, k, :],
                                                    start=(k == 0), stop=(k == QR // P - 1))
                    last.then_inc(weights_used, 1)
                    yield

            def uqp_stage(g0, n):
                wait_mb("uqp", g0)
                for i in range(2):
                    products(g0, n, "w_uq_pe", [i], TT, QR // P, 256)
                    yield
                for i in range(n):
                    yield
                    pe.wait_ge(copied[i], before(("m_copied", "b_copied")[i], "uqp", g0) + 1)
                    pe.wait_ge(t_copied, before("t_copied", "uqp", g0) + i)
                    transposes(qpe[i], H, ROPE).then_inc(t_filled, 1)

            def heads_stage(g, n):
                c = g % NC
                width = (c + 1) * P
                q0 = (g % GROUP) * P
                pair0 = c * HEAD_PAIRS

                def score(k):
                    if k == 0:
                        pe.wait_ge(b_copied, before("b_copied", "heads", g))
                        pe.wait_ge(t_copied, before("t_copied", "heads", g))
                    if pair0 + k:
                        pe.wait_ge(att_exped, 2 * (pair0 + k))
                    for e in range(2):
                        dst, h = B[:, e * 512:e * 512 + width], 2 * k + e
                        nc.tensor.matmul(dst, QT[:, h, q0:q0 + P], KT[:, h, 0:width], start=True, stop=False)
                        last = nc.tensor.matmul(dst, QPT[:, h, q0:q0 + P], KPE[:, 0:width], start=False, stop=True)
                    last.then_inc(att_scored, 1)

                def turn(k):
                    pe.wait_ge(att_normed, pair0 + k + 1)
                    if pair0 + k:
                        pe.wait_ge(att_copied, pair0 + k)
                    for e in range(2):
                        for b in range(c + 1):
                            last = nc.tensor.matmul(T[:, e * 512 + b * P:e * 512 + (b + 1) * P],
                                                    prob[:, k % 2, e, b * P:(b + 1) * P], adiag[:, e, :],
                                                    start=True, stop=True)
                    last.then_inc(att_turned, 1)

                def output(k):
                    pe.wait_ge(att_copied, pair0 + k + 1)
                    if k == 0:
                        pe.wait_ge(m_copied, before("m_copied", "heads", g))
                    for e in range(2):
                        h = 2 * k + e
                        for b in range(c + 1):
                            last = nc.tensor.matmul(M[:, h * P:(h + 1) * P], V[:, b, h * P:(h + 1) * P],
                                                    probT[:, e, b * P:(b + 1) * P], start=(b == 0), stop=(b == c))
                    last.then_inc(att_out, 1)

                for part in range(HEAD_PAIRS + 3):
                    if part >= 3:
                        output(part - 3)
                    if 2 <= part < HEAD_PAIRS + 2:
                        turn(part - 2)
                    if part < HEAD_PAIRS:
                        score(part)
                    yield

            def wo_stage(g0, n):
                wait_mb("wo", g0)
                for i in range(4):
                    products(g0, n, "w_o", [i], TT, DB, 256)
                    yield

            def enorm_stage(g0, n):
                for i in range(n):
                    yield
                    pe.wait_ge(hat_ready, before("hat_ready", "enorm", g0) + i + 1)
                    pe.wait_ge(t_copied, before("t_copied", "enorm", g0) + i)
                    transposes(A[:, i, :], DB).then_inc(t_filled, 1)

            def gates_stage(g0, n):
                pe.wait_ge(t_copied, before("t_copied", "gates", g0))
                wait_mb("gates", g0, n)
                for i in range(4):
                    products(g0, n, "ple_wg", [i], TT, DB, 256)
                    yield

            def add_stage(g0, n):
                pe.wait_ge(pt_loaded, 16 * (EMBED_GROUPS.index(g0) + 1))
                wait_mb("add", g0, n)
                wp = piece("ple_wp", g0, 0)
                for i in range(n):
                    for half in range(2):
                        last = product(MB[i][:, half * 512:half * 512 + 512], pt, i,
                                       wp[:, half * 1024:half * 1024 + 1024], 2, 512)
                last.then_inc(weights_used, 1)
                yield

            stages = dict(pool=pool_stage, fnorm=fnorm_stage, asks=asks_stage, latent=latent_stage, keys=keys_stage,
                          dq=dq_stage, uq=uq_stage, uqp=uqp_stage, heads=heads_stage, wo=wo_stage,
                          enorm=enorm_stage, gates=gates_stage, add=add_stage)

            def zero_sums(g, start, stop):
                for half in range(2):
                    last = nc.tensor.matmul(acc[:, half * 512:half * 512 + 512], zeros[:], HP[:, g % HPB, 0:512],
                                            start=start, stop=stop)
                return last

            def open_pair(g):
                if g == 0:
                    zero_sums(g, True, False).then_inc(slots_free, NPE)

            def reopen(g):
                pe.wait_ge(x_ready, before("x_ready", "residual", g - 1) + 1)
                zero_sums(g, True, False)

            def gather_bodies(g, j, count):
                if g and j == 0:
                    reopen(g)
                first = g * BODIES + j

                def body(it):
                    for p, s in enumerate(PE_SLOTS):
                        pe.wait_ge(diag_ready, it * NPE + (first * NPE + p + 1))
                        for half in range(2):
                            last = nc.tensor.matmul(acc[:, half * 512:half * 512 + 512], diag[s][:],
                                                    slot[s][:, D + half * 512:D + half * 512 + 512],
                                                    start=False, stop=False)
                        last.then_inc(slots_free, 1)

                run_bodies(pe, count, body)

            def close_pair(g):
                zero_sums(g, False, True).then_inc(acc_done, 1)

            pe.wait_ge(const_loaded, 16 * CONSTS)
            pe.wait_ge(zeroed, 1)
            run_between(stages, gather_bodies, open_pair, close_pair)

        @block.scalar
        def _(act):
            def norm(stage, g0, src, width, i=0):
                n = norm_number(stage, g0, i)
                nc.scalar.activation(sq_out[:, 0:width], src, ACT.Square, accum_out=ss[:, n:n + 1]
                                     ).then_inc(squared, 1)
                act.wait_ge(squared, n + 1)
                nc.scalar.activation(rms[:, n:n + 1], ss[:, n:n + 1], ACT.Sqrt, bias=eps, scale=1.0 / width
                                     ).then_inc(normed, 1)

            def pool_stage(g0, n):
                for i in range(n):
                    act.wait_ge(x_loaded[g0 + i], 16)
                    norm("pool", g0, X[:, g0 + i, :], D, i)
                for i in range(n):
                    yield
                    yield
                    act.wait_ge(t_filled, before("t_filled", "pool", g0) + i + 1)
                    if i:
                        act.wait_ge(pooled, before("pooled", "pool", g0) + i)
                    nc.scalar.activation(TU[:, :, 0:P], T[:, :].rearrange(blocks, t=P), ACT.Copy).then_inc(t_copied, 1)

            def fnorm_stage(g0, n):
                act.wait_ge(x_ready, before("x_ready", "fnorm", g0))
                for i in range(n):
                    norm("fnorm", g0, X[:, (g0 + i) % NC, :], D, i)
                yield
                for i in range(n):
                    yield
                    act.wait_ge(t_filled, before("t_filled", "fnorm", g0) + i + 1)
                    nc.scalar.activation(TT[:, :, i * P:(i + 1) * P], T[:, :].rearrange(blocks, t=P), ACT.Copy
                                         ).then_inc(t_copied, 1)

            def asks_stage(g0, n):
                for p in range(PH):
                    yield
                    act.wait_ge(weights_used, used("wq", g0, p))
                    if p >= 2:
                        act.wait_ge(t_filled, before("t_filled", "asks", g0) + p - 1)
                    nc.scalar.activation(asked[:, p % 2, :, 0:n * P],
                                         (B, M)[p % 2][:, :].rearrange("p (e t) -> p e t", e=2)[:, :, 0:n * P],
                                         ACT.Copy).then_inc((b_copied, m_copied)[p % 2], 1)

            def select_stage(g, n):
                yield
                act.wait_ge(gate_shifted, g + 1)
                nc.scalar.activation(shifted[:, :, :], shifted[:, :, :], ACT.Exp).then_inc(gate_exped, 1)

            def latent_stage(g0, n):
                act.wait_ge(x_ready, before("x_ready", "latent", g0))
                for i in range(n):
                    norm("latent", g0, X[:, (g0 + i) % NC, :], D, i)
                for _ in range(4):
                    yield
                act.wait_ge(weights_used, used("w_dkv", g0, 0))
                for i in range(n):
                    norm("latent", g0, MB[i][:, 0:KVR], KVR, n + i)

            def keys_stage(g0, n):
                c = g0 % NC
                yield
                act.wait_ge(weights_used, used("w_ukv_k", g0, 0))
                for i in range(2):
                    nc.scalar.activation(KT[:, 4 * i:4 * i + 4, c * P:(c + 2) * P], MB[i][:, :].rearrange(blocks, t=W2),
                                         ACT.Copy).then_inc(copied[i], 1)
                yield
                act.wait_ge(weights_used, used("w_ukv_v", g0, 0))
                for i in range(n):
                    nc.scalar.activation(V[:, c + i, :], MB[i][:, :], ACT.Copy).then_inc(copied[i], 1)

            def dq_stage(g0, n):
                for _ in range(3):
                    yield
                act.wait_ge(weights_used, used("w_dq", g0, 2))
                for i in range(n):
                    norm("dq", g0, MB[i][:, 0:QR], QR, i)

            def uq_stage(g0, n):
                for half in range(2):
                    yield
                    yield
                    act.wait_ge(weights_used, used("w_uq_nope", g0, 2 * half + 1))
                    nc.scalar.activation(QT[:, 4 * half:4 * half + 4, :], MB[half][:, :].rearrange(blocks, t=W2),
                                         ACT.Copy).then_inc(copied[half], 1)

            def uqp_stage(g0, n):
                for _ in range(3):
                    yield
                for i in range(n):
                    yield
                    act.wait_ge(t_filled, before("t_filled", "uqp", g0) + i + 1)
                    nc.scalar.activation(QPT[:, :, i * P:(i + 1) * P], T[0:ROPE, :].rearrange(blocks, t=P), ACT.Copy
                                         ).then_inc(t_copied, 1)

            def heads_stage(g, n):
                c = g % NC
                width = (c + 1) * P
                pair0 = c * HEAD_PAIRS
                at = (g % GROUP) * P

                def copy(k):
                    act.wait_ge(att_turned, pair0 + k + 1)
                    if pair0 + k:
                        act.wait_ge(att_out, pair0 + k)
                    nc.scalar.activation(probT[:, :, 0:width], T[:, :].rearrange("p (e s) -> p e s", e=2)[:, :, 0:width],
                                         ACT.Copy).then_inc(att_copied, 1)

                def exp(k):
                    act.wait_ge(att_maxed, pair0 + k + 1)
                    for e in range(2):
                        n = c * H + 2 * k + e
                        nc.scalar.activation(prob[:, k % 2, e, 0:width], B[:, e * 512:e * 512 + width], ACT.Exp,
                                             bias=nmax[:, n:n + 1], scale=SCALE, accum_out=asum[:, n:n + 1]
                                             ).then_inc(att_exped, 1)

                for part in range(HEAD_PAIRS + 4):
                    if 3 <= part < HEAD_PAIRS + 3:
                        copy(part - 3)
                    if 1 <= part < HEAD_PAIRS + 1:
                        exp(part - 1)
                    if part >= 5 and part % 2:
                        half = (part - 5) // 2
                        act.wait_ge(att_out, pair0 + 2 * half + 2)
                        nc.scalar.activation(TT[:, 4 * half:4 * half + 4, at:at + P],
                                             M[:, half * 512:half * 512 + 512].rearrange(blocks, t=P), ACT.Copy
                                             ).then_inc(m_copied, 1)
                    if part < HEAD_PAIRS + 3:
                        yield

            def enorm_stage(g0, n):
                act.wait_ge(x_ready, before("x_ready", "enorm", g0))
                for i in range(n):
                    norm("enorm", g0, X[:, (g0 + i) % NC, :], D, i)
                yield

            def gates_stage(g0, n):
                for _ in range(4):
                    yield
                act.wait_ge(weights_used, used("ple_wg", g0, 3))
                for i in range(n):
                    nc.scalar.activation(A[:, i, :], MB[i][:, :], ACT.Sigmoid).then_inc(copied[i], 1)

            def add_stage(g0, n):
                yield
                yield
                if g0 >= NC:
                    for i in range(n):
                        act.wait_ge(x_ready, before("x_ready", "add", g0) + i + 1)
                        norm("add", g0, X[:, (g0 + i) % NC, :], D, i)
                    for i in range(n):
                        c = (g0 + i) % NC
                        act.wait_ge(out_ready, c + 1)
                        act.dma_start(out[c * P:(c + 1) * P, :], outs[c]).then_inc(out_stored, 16)

            stages = dict(pool=pool_stage, fnorm=fnorm_stage, asks=asks_stage, select=select_stage,
                          latent=latent_stage, keys=keys_stage, dq=dq_stage, uq=uq_stage, uqp=uqp_stage,
                          heads=heads_stage, enorm=enorm_stage, gates=gates_stage, add=add_stage)

            def gather_bodies(g, j, count):
                first = g * BODIES + j
                nb = SLOTS // BATCH

                def body(it):
                    for b in range(nb):
                        at = slice(b * BATCH, (b + 1) * BATCH)
                        act.wait_ge(dotted, it * SLOTS + (first * SLOTS + (b + 1) * BATCH))
                        nc.scalar.activation(act_a[:, at], a[:, at], ACT.Gelu_apprx_tanh).then_inc(gelued, 1)
                        act.wait_ge(weighted, it * nb + (first * nb + b + 1))
                        for p, s in enumerate(PE_SLOTS):
                            if s // BATCH == b:
                                act.wait_ge(slots_free, it * NPE + (first * NPE + p + 1))
                                nc.scalar.activation(diag[s][:], ident, ACT.Copy, scale=w[:, s:s + 1]
                                                     ).then_inc(diag_ready, 1)

                run_bodies(act, count, body)

            act.wait_ge(const_loaded, 16 * CONSTS)
            act.wait_ge(trig_shifted, 1)
            nc.scalar.activation(cs[:, :, :, :], cs[:, :, :, :], ACT.Sin).then_inc(trig_done, 1)
            run_between(stages, gather_bodies)
            act.wait_ge(out_stored, 16 * NC)

        @block.vector
        def _(dve):
            steps = [0]

            def step(ins):
                ins.then_inc(dve_steps, 1)
                steps[0] += 1

            def settle():
                dve.wait_ge(dve_steps, steps[0])

            def reciprocal_rms(stage, g0, i=0):
                n = norm_number(stage, g0, i)
                dve.wait_ge(normed, n + 1)
                step(nc.vector.reciprocal(rstd[:, n:n + 1], rms[:, n:n + 1]))
                settle()
                return rstd[:, n:n + 1]

            def columns(at, n):
                return gc[:, at:at + n].unsqueeze(2).broadcast_to([P, n, P])

            def pool_stage(g0, n):
                def mix(i):
                    g = g0 + i
                    r = reciprocal_rms("pool", g0, i)
                    if g >= 2:
                        dve.wait_ge(t_filled, before("t_filled", "pool", g0) + i)
                    nc.vector.scalar_tensor_tensor(hpool[:, g % 2, :], X[:, g, :], r, mix_gain, ALU.mult, ALU.mult
                                                   ).then_inc(mixed, 1)

                def add(i):
                    g = g0 + i
                    if i < n - 1:
                        dve.wait_ge(pooled, before("pooled", "pool", g0) + i + 1)
                    else:
                        dve.wait_ge(weights_used, used("pool_w", g0, 0))
                    step(nc.vector.tensor_tensor(SD[:, 0:D], M[:, :], pool_scale, ALU.mult))
                    settle()
                    nc.vector.tensor_tensor(X[:, g, :], X[:, g, :], SD[:, 0:D], ALU.add).then_inc(x_ready, 1)

                mix(0)
                for i in range(n):
                    yield
                    if i:
                        add(i - 1)
                    yield
                    if i < n - 1:
                        mix(i + 1)
                yield
                add(n - 1)

            def fnorm_stage(g0, n):
                yield
                for i in range(n):
                    g = g0 + i
                    r = reciprocal_rms("fnorm", g0, i)
                    if g == NC:
                        dve.wait_ge(gain_loaded, 16)
                    nc.vector.scalar_tensor_tensor(HP[:, g % HPB, :], X[:, g % NC, :], r, gain[:, :], ALU.mult, ALU.mult
                                                   ).then_inc(hp_ready, 1)

            def top16(n, values, left, tops, places):
                for i in range(n):
                    step(nc.vector.max(tops(i)[:, 0:8], values(i)))
                settle()
                for i in range(n):
                    step(nc.vector.match_replace(left(i), tops(i)[:, 0:8], values(i), LOW))
                    step(nc.vector.max_index(places(i)[:, 0:8], tops(i)[:, 0:8], values(i)))
                settle()
                for i in range(n):
                    step(nc.vector.max(tops(i)[:, 8:16], left(i)))
                settle()
                for i in range(n):
                    last = nc.vector.max_index(places(i)[:, 8:16], tops(i)[:, 8:16], left(i))
                    if i < n - 1:
                        step(last)
                return last

            def asks_stage(g0, n):
                yield
                for p in range(PH):
                    yield
                    dve.wait_ge(t_filled, before("t_filled", "asks", g0) + p + 1)
                    j = p % 2
                    top16(2 * n, lambda r: T[:, j * 512 + r * P:j * 512 + (r + 1) * P],
                          lambda r: SD[:, j * D + r * P:j * D + (r + 1) * P],
                          lambda r: top[:, r // 2, p, r % 2, :],
                          lambda r: top_u[:, r // 2, p, r % 2, :]).then_inc(t_copied, 1)

            def pick_stage(g, n):
                i = PLACE[g]
                dve.wait_ge(t_copied, before("t_copied", "pick", g))
                step(nc.vector.tensor_copy(top_i[:, :, :, :], top_u[:, i, :, :, :]))
                cand = SC[:, :].rearrange("p (h i j) -> p h i j", h=PH, i=TOPK)
                n2 = TOPK * TOPK
                for h0 in (0, PH // 2):
                    hs = slice(h0, h0 + PH // 2)
                    step(nc.vector.tensor_tensor(
                        cand[:, hs], top[:, i, hs, 0, :].unsqueeze(3).broadcast_to([P, PH // 2, TOPK, TOPK]),
                        top[:, i, hs, 1, :].unsqueeze(2).broadcast_to([P, PH // 2, TOPK, TOPK]), ALU.add))
                    settle()
                    step(top16(PH // 2, lambda h: SC[:, (h0 + h) * n2:(h0 + h + 1) * n2],
                               lambda h: SD[:, (h0 + h) * n2:(h0 + h + 1) * n2],
                               lambda h: best[:, h0 + h, :], lambda h: pos_u[:, h0 + h, :]))
                    settle()
                    if h0 == 0:
                        yield

            def select_stage(g, n):
                nc.vector.tensor_tensor(shifted[:, :, :], best[:, :, :], best[:, :, 0:1].broadcast_to([P, PH, TOPK]),
                                        ALU.subtract).then_inc(gate_shifted, 1)
                flat = pos_u[:, :, :].rearrange("p h k -> p (h k)")
                step(nc.vector.tensor_scalar(half_u[:, 0, :], flat, 4, None, ALU.logical_shift_right))
                step(nc.vector.tensor_scalar(half_u[:, 1, :], flat, TOPK - 1, None, ALU.bitwise_and))
                settle()
                step(nc.vector.tensor_copy(half_f[:, :, :], half_u[:, :, :]))
                settle()
                onehot = [SC, SD]
                for p in range(2):
                    step(nc.vector.tensor_tensor(
                        onehot[p][:, :].rearrange("p (n j) -> p n j", j=TOPK),
                        half_f[:, p, :].unsqueeze(2).broadcast_to([P, KSEL, TOPK]),
                        iota.unsqueeze(1).broadcast_to([P, KSEL, TOPK]), ALU.is_equal))
                    settle()
                    v = onehot[p][:, :].rearrange("p (h k j) -> p h k j", h=PH, k=TOPK)
                    step(nc.vector.tensor_tensor(
                        v, v, top_i[:, :, p, :].unsqueeze(2).broadcast_to([P, PH, TOPK, TOPK]), ALU.mult))
                    settle()
                    step(nc.vector.reduce_sum(half_f[:, p, :], onehot[p][:, :].rearrange("p (n j) -> p n j", j=TOPK),
                                              axis=AX))
                    settle()
                    if p == 0:
                        yield
                nc.vector.scalar_tensor_tensor(idx[:, g % HPB, :], half_f[:, 0, :], float(P), half_f[:, 1, :],
                                               ALU.mult, ALU.add).then_inc(idx_ready, 1)
                yield
                dve.wait_ge(gate_exped, g + 1)
                step(nc.vector.reduce_sum(gsum[:, :], shifted[:, :, :], axis=AX))
                settle()
                step(nc.vector.reciprocal(grec[:, :], gsum[:, :]))
                settle()
                step(nc.vector.tensor_tensor(gate[:, g % HPB, :].rearrange("p (h k) -> p h k", h=PH), shifted[:, :, :],
                                             grec[:, :].unsqueeze(2).broadcast_to([P, PH, TOPK]), ALU.mult))
                settle()

            def rope(dst, src, heads, c, tmp):
                def bc(i):
                    return cs[:, i, c, :].unsqueeze(1).broadcast_to([P, heads, HALF])
                s3 = src.rearrange("p (h d) -> p h d", h=heads)
                d3 = dst.rearrange("p (h d) -> p h d", h=heads)
                n = heads * HALF
                t3 = tmp[:, 0:n].rearrange("p (h d) -> p h d", h=heads)
                u3 = tmp[:, 256:256 + n].rearrange("p (h d) -> p h d", h=heads)
                lo, hi = slice(0, HALF), slice(HALF, ROPE)
                step(nc.vector.tensor_tensor(d3[:, :, lo], s3[:, :, lo], bc(0), ALU.mult))
                step(nc.vector.tensor_tensor(t3, s3[:, :, hi], bc(1), ALU.mult))
                step(nc.vector.tensor_tensor(d3[:, :, hi], s3[:, :, hi], bc(0), ALU.mult))
                step(nc.vector.tensor_tensor(u3, s3[:, :, lo], bc(1), ALU.mult))
                settle()
                step(nc.vector.tensor_tensor(d3[:, :, lo], d3[:, :, lo], t3, ALU.subtract))
                return nc.vector.tensor_tensor(d3[:, :, hi], d3[:, :, hi], u3, ALU.add)

            def latent_stage(g0, n):
                c, t0 = g0 % NC, before("t_filled", "latent", g0)
                yield
                for i in range(n):
                    r = reciprocal_rms("latent", g0, i)
                    nc.vector.tensor_scalar(A[:, i, :], X[:, c + i, :], r, None, ALU.mult).then_inc(hat_ready, 1)
                for i in range(n):
                    yield
                    dve.wait_ge(t_filled, t0 + i + 1)
                    at = slice(i * P, (i + 1) * P)
                    tv = T[:, :].rearrange(blocks, t=P)
                    nc.vector.tensor_tensor(TU[:, :, at], tv, columns(G_KV, DB), ALU.mult)
                    nc.vector.tensor_tensor(TT[:, :, at], tv, columns(G_MIX1, DB), ALU.mult).then_inc(t_copied, 1)
                yield
                dve.wait_ge(weights_used, used("w_dkv", g0, 1))
                if g0 == NC:
                    dve.wait_ge(trig_done, 1)
                for i in range(n):
                    step(rope(kpe[i], MB[i][:, 512:512 + ROPE], 1, c + i, rtmp))
                    settle()
                yield
                for i in range(n):
                    r = reciprocal_rms("latent", g0, n + i)
                    nc.vector.tensor_scalar(ckv[i], MB[i][:, 0:KVR], r, None, ALU.mult).then_inc(copied[i], 1)
                yield
                dve.wait_ge(t_filled, t0 + n + 1)
                ti = T[:, :].rearrange("p (i b t) -> p i b t", i=2, b=4)
                nc.vector.tensor_tensor(
                    ckvT.rearrange("p b (i t) -> p i b t", i=2), ti[:, :, 0:2, :],
                    gc[:, G_CKV:G_CKV + 2].unsqueeze(1).unsqueeze(3).broadcast_to([P, 2, 2, P]), ALU.mult)
                nc.vector.tensor_copy(KPE[:, c * P:(c + 2) * P].rearrange("p (i t) -> p i t", i=2), ti[0:ROPE, :, 2, :]
                                      ).then_inc(t_copied, 1)

            def dq_stage(g0, n):
                for _ in range(4):
                    yield
                for i in range(n):
                    r = reciprocal_rms("dq", g0, i)
                    nc.vector.tensor_scalar(A[:, i, 0:QR], MB[i][:, 0:QR], r, None, ALU.mult).then_inc(copied[i], 1)
                nb = QR // P
                for i in range(n):
                    yield
                    dve.wait_ge(t_filled, before("t_filled", "dq", g0) + i + 1)
                    nc.vector.tensor_tensor(TT[:, 0:nb, i * P:(i + 1) * P], T[:, 0:QR].rearrange(blocks, t=P),
                                            columns(G_Q, nb), ALU.mult).then_inc(t_copied, 1)

            def uqp_stage(g0, n):
                yield
                yield
                dve.wait_ge(weights_used, used("w_uq_pe", g0, 1))
                for i in range(n):
                    if i:
                        settle()
                        dve.wait_ge(copied[i - 1], before(("m_copied", "b_copied")[i - 1], "uqp", g0) + 1)
                    rope(qpe[i], MB[i][:, 0:H * ROPE], H, g0 % NC + i, rtmp).then_inc(copied[i], 1)

            def heads_stage(g, n):
                c = g % NC
                width = (c + 1) * P
                pair0 = c * HEAD_PAIRS

                def largest(k):
                    s = B[:, :].rearrange("p (e s) -> p e s", e=2)
                    m = c * H + 2 * k
                    dve.wait_ge(att_scored, pair0 + k + 1)
                    step(nc.vector.tensor_tensor(s[:, :, c * P:width], s[:, :, c * P:width],
                                                 mask.unsqueeze(1).broadcast_to([P, 2, P]), ALU.add))
                    settle()
                    step(nc.vector.reduce_max(amax[:, m:m + 2], s[:, :, 0:width], axis=AX))
                    settle()
                    nc.vector.tensor_scalar(nmax[:, m:m + 2], amax[:, m:m + 2], -SCALE, None, ALU.mult
                                            ).then_inc(att_maxed, 1)

                def diagonal(k):
                    m = c * H + 2 * k
                    dve.wait_ge(att_exped, m + 2)
                    step(nc.vector.reciprocal(arec[:, m:m + 2], asum[:, m:m + 2]))
                    settle()
                    if pair0 + k:
                        dve.wait_ge(att_turned, pair0 + k)
                    nc.vector.tensor_tensor(adiag, ident.unsqueeze(1).broadcast_to([P, 2, P]),
                                            arec[:, m:m + 2].unsqueeze(2).broadcast_to([P, 2, P]), ALU.mult
                                            ).then_inc(att_normed, 1)

                for part in range(HEAD_PAIRS + 2):
                    if part >= 2:
                        diagonal(part - 2)
                    if 1 <= part < HEAD_PAIRS + 1:
                        largest(part - 1)
                    yield

            def wo_stage(g0, n):
                for _ in range(4):
                    yield
                dve.wait_ge(weights_used, used("w_o", g0, 3))
                for i in range(n):
                    c = (g0 + i) % NC
                    nc.vector.tensor_tensor(X[:, c, :], X[:, c, :], MB[i][:, :], ALU.add).then_inc(x_ready, 1)

            def residual_stage(g, n):
                dve.wait_ge(acc_done, g + 1)
                dve.wait_ge(v_added, NDVE * (1 + (g + 1) * BODIES))
                nc.vector.tensor_tensor(X[:, g % NC, :], X[:, g % NC, :], acc[:, :], ALU.add).then_inc(x_ready, 1)
                yield

            def enorm_stage(g0, n):
                yield
                for i in range(n):
                    r = reciprocal_rms("enorm", g0, i)
                    nc.vector.tensor_scalar(A[:, i, :], X[:, (g0 + i) % NC, :], r, None, ALU.mult).then_inc(hat_ready, 1)
                for i in range(n):
                    yield
                    dve.wait_ge(t_filled, before("t_filled", "enorm", g0) + i + 1)
                    nc.vector.tensor_tensor(TT[:, :, i * P:(i + 1) * P], T[:, :].rearrange(blocks, t=P),
                                            columns(G_PLE + (g0 // NC) * DB, DB), ALU.mult).then_inc(t_copied, 1)

            def add_stage(g0, n):
                yield
                dve.wait_ge(weights_used, used("ple_wp", g0, 0))
                for i in range(n):
                    name = ("m_copied", "b_copied")[i]
                    dve.wait_ge(copied[i], before(name, "add", g0))
                    nc.vector.tensor_tensor(A[:, i, :], A[:, i, :], MB[i][:, :], ALU.mult).then_inc(copied[i], 1)
                for i in range(n):
                    c, name = (g0 + i) % NC, ("m_copied", "b_copied")[i]
                    dve.wait_ge(copied[i], before(name, "add", g0) + 1)
                    nc.vector.tensor_tensor(X[:, c, :], X[:, c, :], A[:, i, :], ALU.add).then_inc(x_ready, 1)
                if g0 >= NC:
                    yield
                    yield
                    if g0 == NC:
                        dve.wait_ge(gain_loaded, 32)
                    for i in range(n):
                        c = (g0 + i) % NC
                        r = reciprocal_rms("add", g0, i)
                        nc.vector.scalar_tensor_tensor(outs[c], X[:, c, :], r, gain[:, :], ALU.mult, ALU.mult
                                                       ).then_inc(out_ready, 1)

            stages = dict(pool=pool_stage, fnorm=fnorm_stage, asks=asks_stage, pick=pick_stage, select=select_stage,
                          latent=latent_stage, dq=dq_stage, uqp=uqp_stage, heads=heads_stage, wo=wo_stage,
                          residual=residual_stage, enorm=enorm_stage, add=add_stage)

            def gather_bodies(g, j, count):
                first = g * BODIES + j
                nb = SLOTS // BATCH
                Xc = X[:, g % NC, :]

                def body(it):
                    for b in range(nb):
                        for s in range(b * BATCH, (b + 1) * BATCH):
                            dve.wait_ge(rows_loaded[s], it * 16 + 16 * (first + 1))
                            nc.vector.tensor_tensor_reduce(
                                out=slot[s][:, 0:D], in0=slot[s][:, 0:D], in1=HP[:, g % HPB, :], scale=1.0, scalar=0.0,
                                op0=ALU.mult, op1=ALU.add, accum_out=a[:, s:s + 1]).then_inc(dotted, 1)
                        at = slice(b * BATCH, (b + 1) * BATCH)
                        dve.wait_ge(gelued, it * nb + (first * nb + b + 1))
                        nc.vector.tensor_tensor(
                            w[:, at], act_a[:, at],
                            gate[:, g % HPB, bass.ds(it * SLOTS + (j * SLOTS + b * BATCH), BATCH)], ALU.mult
                        ).then_inc(weighted, 1)
                        dve.wait_ge(weighted, it * nb + (first * nb + b + 1))
                        for d, s in enumerate(DVE_SLOTS):
                            if s // BATCH == b:
                                dve.wait_ge(v_added, it * NDVE + (first * NDVE + NDVE + d))
                                nc.vector.scalar_tensor_tensor(Xc, slot[s][:, D:2 * D], w[:, s:s + 1], Xc,
                                                               ALU.mult, ALU.add).then_inc(v_added, 1)

                run_bodies(dve, count, body)

            nc.vector.memset(zeros[:], 0.0).then_inc(zeroed, 1)
            nc.vector.memset(w[:], 0.0).then_inc(v_added, NDVE)
            dve.wait_ge(const_loaded, 16 * CONSTS)
            step(nc.vector.tensor_copy(pos_f[:], pos_i[:]))
            settle()
            angle, turns = SC[:, 0:NC * HALF], SC[:, 512:512 + NC * HALF]
            magic = float(np.float32(1.5 * 2 ** 23))
            part1 = 6.28125
            part2 = float(np.float32(np.float32(0.0019350051879882812)))
            part3 = float(np.float32(2 * np.pi - part1 - part2))
            for c in range(NC):
                step(nc.vector.tensor_scalar(angle[:, c * HALF:(c + 1) * HALF], inv, pos_f[:, c:c + 1], None, ALU.mult))
            settle()
            for i, ahead in ((0, 0.25), (1, 0.0)):
                dst = cs[:, i, :, :].rearrange("p c d -> p (c d)")
                step(nc.vector.tensor_scalar(turns, angle, float(1 / (2 * np.pi)), ahead, ALU.mult, ALU.add))
                settle()
                step(nc.vector.tensor_scalar(turns, turns, magic, None, ALU.add))
                settle()
                step(nc.vector.tensor_scalar(turns, turns, -magic, None, ALU.add))
                settle()
                step(nc.vector.scalar_tensor_tensor(dst, turns, -part1, angle, ALU.mult, ALU.add))
                settle()
                step(nc.vector.scalar_tensor_tensor(dst, turns, -part2, dst, ALU.mult, ALU.add))
                settle()
                step(nc.vector.scalar_tensor_tensor(dst, turns, -part3, dst, ALU.mult, ALU.add))
                settle()
                step(nc.vector.tensor_scalar(dst, dst, float(np.pi / 2) if ahead else 0.0, float(np.float32(3.1415925)),
                                             ALU.add, ALU.min))
                settle()
                last = nc.vector.tensor_scalar(dst, dst, -float(np.float32(3.1415925)), None, ALU.max)
                if i == 0:
                    step(last)
                    settle()
            last.then_inc(trig_shifted, 1)

            run_between(stages, gather_bodies)


def shape_constants():
    t = np.arange(P)
    c = np.zeros((P, C_WIDTH), np.float32)
    c[:, C_IDENT:C_IDENT + P] = np.eye(P)
    c[:, C_MASK:C_MASK + P] = np.where(t[None, :] <= t[:, None], 0.0, -1.0e30)
    c[:, C_IOTA:C_IOTA + TOPK] = np.arange(TOPK)
    c[:, C_INV:C_INV + HALF] = np.float32(10000.0) ** (-np.arange(0, ROPE, 2, dtype=np.float32) / ROPE)
    c[:, C_EPS] = EPS
    pools = np.zeros((P, 3, len(WINDOWS), P), np.float32)
    for n, w in enumerate(WINDOWS):
        d = t[None, :] - t[:, None]
        inside = (d >= 0) & (d < w)
        pools[:, 0, n] = inside / np.minimum(t + 1, w)[None, :] - np.eye(P)
        pools[:, 1, n] = inside / w - np.eye(P)
        pools[:, 2, n] = (d + P < w) / w
    return c, pools.reshape(P, -1)


def by_columns(w, cols):
    k, n = w.shape
    return np.ascontiguousarray(w.reshape(k // P, P, n // cols, cols).transpose(2, 1, 0, 3).reshape(n // cols, P, -1))


def by_halves(w):
    return by_columns(w, 512).transpose(1, 0, 2).reshape(1, P, -1)


def kernel(x, p, positions, mix_norm, ffn_norm, pool_w, pool_scale, kv_in_norm, w_dkv, kv_norm, w_ukv,
           w_dq, q_norm, w_uq, w_o, peer_wq, peer_keys, peer_u, peer_v, ple_norm, ple_wg, ple_wp, final_norm):
    import concourse.bacc as bacc
    from concourse.bass_utils import run_bass_kernel_spmd as run

    (x, p, positions, mix_norm, ffn_norm, pool_w, pool_scale, kv_in_norm, w_dkv, kv_norm, w_ukv, w_dq, q_norm, w_uq,
     w_o, peer_wq, peer_keys, peer_u, peer_v, ple_norm, ple_wg, ple_wp, final_norm) = (
        np.asarray(v) for v in (
            x, p, positions, mix_norm, ffn_norm, pool_w, pool_scale, kv_in_norm, w_dkv, kv_norm, w_ukv, w_dq, q_norm,
            w_uq, w_o, peer_wq, peer_keys, peer_u, peer_v, ple_norm, ple_wg, ple_wp, final_norm))

    consts, pools = shape_constants()
    arrays = {
        "consts": consts,
        "pools": pools,
        "gcols": np.concatenate([v.reshape(-1, P).T for v in (kv_in_norm, mix_norm[1], ple_norm[0], ple_norm[1],
                                                              kv_norm, q_norm[0])], axis=1),
        "gains": np.stack([mix_norm[0], pool_scale[0], ffn_norm[0], ffn_norm[1], final_norm]),
        "positions": positions.reshape(NC, P).T,
        "x": x.reshape(S, D),
        "pT": p.reshape(DEPTH, S, PLE // P, P).transpose(0, 3, 2, 1),
    }
    for l in range(DEPTH):
        arrays[f"uv{l}"] = np.concatenate([peer_u[l], peer_v[l]], axis=1)
    heads_kv = w_ukv.reshape(KVR, H, NOPE + VH)
    heads_q = w_uq[0].reshape(QR, H, NOPE + ROPE)
    per_layer = {
        ("pool_w", 0): pool_w[0].reshape(len(WINDOWS), 2, P, GW).transpose(2, 0, 1, 3).reshape(1, P, -1),
        ("w_ukv_k", 1): by_columns(heads_kv[:, :, :NOPE].reshape(KVR, -1), H * NOPE),
        ("w_ukv_v", 1): by_halves(heads_kv[:, :, NOPE:].reshape(KVR, -1)),
        ("w_dq", 1): by_columns(w_dq[0], 256),
        ("w_uq_nope", 1): by_columns(heads_q[:, :, :NOPE].reshape(QR, -1), 256),
        ("w_uq_pe", 1): by_columns(heads_q[:, :, NOPE:].reshape(QR, -1), 256),
        ("w_o", 1): by_columns(w_o[0], 256),
    }
    for l in range(DEPTH):
        per_layer["wq", l] = by_columns(peer_wq[l], 256)
        arrays[f"keys{l}"] = peer_keys[l].reshape(2 * PH, P, P).transpose(2, 0, 1).reshape(P, DB, -1)
        per_layer["ple_wg", l] = by_columns(ple_wg[l], 256)
        per_layer["ple_wp", l] = by_halves(ple_wp[l])
    for (name, l), v in per_layer.items():
        arrays[f"{name}_{l}"] = v
    arrays["w_dkv_a"] = by_columns(w_dkv[:, :KVR], KVR)
    arrays["w_dkv_b"] = by_columns(w_dkv[:, KVR:], ROPE)
    arrays = {n: np.ascontiguousarray(v) for n, v in arrays.items()}

    nc = bacc.Bacc("TRN2", target_bir_lowering=False, num_devices=1)
    ap = {n: nc.dram_tensor(f"in_{n}", v.shape, mybir.dt.from_np(v.dtype), kind="ExternalInput").ap()
          for n, v in arrays.items()}
    out = nc.dram_tensor("out", (S, D), F32, kind="ExternalOutput").ap()
    weights = {(name, l): [ap[f"{name}_{l}"][i] for i in range(v.shape[0])] for (name, l), v in per_layer.items()}
    weights["w_dkv", 1] = [ap["w_dkv_a"][0], ap["w_dkv_b"][0]]
    trunk(nc, ap["consts"], ap["pools"], ap["gcols"], ap["gains"], ap["positions"], ap["x"], ap["pT"],
          [ap["uv0"], ap["uv1"]], weights, [ap["keys0"], ap["keys1"]], out)
    r = run(nc, [{f"in_{n}": v for n, v in arrays.items()}], core_ids=[0])
    return r.results[0]["out"].reshape(1, S, D)
```

```python
import numpy as np
import concourse.bass as bass
from concourse import mybir
from contextlib import ExitStack

F32 = mybir.dt.float32
BF16 = mybir.dt.bfloat16
I32 = mybir.dt.int32
U32 = mybir.dt.uint32
ALU = mybir.AluOpType
ACT = mybir.ActivationFunctionType
AX = mybir.AxisListType.X

P = 128
S, D, DEPTH = 512, 1024, 2
NC = S // P
DB = D // P
PAIRS = DEPTH * NC
WINDOWS = (2, 4, 8, 16)
GW = D // len(WINDOWS)
H, NOPE, ROPE, VH = 8, 128, 64, 128
HEAD_PAIRS = H // 2
HALF = ROPE // 2
QR, KVR = 768, 256
SCALE = 1.0 / float(np.sqrt(NOPE + ROPE))
PH, TOPK = 8, 16
KSEL = PH * TOPK
NEXP = P * P
PLE = 256
EPS = 1e-6
LOW = -3.0e38

RING = 2
PIECE = 2048
GROUP = 2
SLOTS = 8
BATCH = 4
BODIES = KSEL // SLOTS
NB = SLOTS // BATCH
UNITS = KSEL // BATCH
DVE_SLOTS = (3, 6, 7)
PE_SLOTS = tuple(s for s in range(SLOTS) if s not in DVE_SLOTS)
NPE, NDVE = len(PE_SLOTS), len(DVE_SLOTS)
HPB = 3

C_IDENT, C_MASK, C_IOTA, C_INV, C_EPS = 0, P, 2 * P, 2 * P + TOPK, 2 * P + TOPK + HALF
C_WIDTH = C_EPS + 1
G_KV, G_MIX1, G_PLE, G_CKV, G_Q = 0, DB, 2 * DB, 4 * DB, 4 * DB + KVR // P
G_WIDTH = G_Q + QR // P


def stages_of(names, g0, n):
    return [(name, g0, n) for name in names]


def rank(g, half):
    return stages_of([f"rank{half}"], g, 1)


def embed(g0, n):
    return stages_of(["enorm", "gates", "add"], g0, n)


def residual(g):
    return stages_of(["residual"], g, 1)


def ask_first(g0, n):
    return stages_of(["fnorm", "asks0"], g0, n) + rank(g0, 0)


def ask_second(g0, n):
    return stages_of(["asks1"], g0, n)


def keys_values(g0):
    return stages_of(["latent", "keys", "dq", "uq"], g0, 2)


def attention(g0):
    return (stages_of(["uqp"], g0, 2) + stages_of(["heads"], g0, 1) + stages_of(["heads"], g0 + 1, 1) +
            stages_of(["wo"], g0, 2))


START = stages_of(["pool"], 0, 1) + ask_first(0, 1)
STEPS = [
    (ask_second(0, 1) + stages_of(["pool"], 1, 1) + stages_of(["pool"], 2, 2) + ask_first(1, 1) +
     stages_of(["trig"], 0, 1)),
    residual(0) + ask_second(1, 1) + ask_first(2, 2),
    residual(1) + ask_second(2, 2) + embed(0, 2) + keys_values(4),
    residual(2) + attention(4) + ask_first(4, 2),
    residual(3) + ask_second(4, 2) + embed(2, 2) + keys_values(6),
    residual(4) + attention(6) + ask_first(6, 2),
    residual(5) + ask_second(6, 2) + embed(4, 2),
    residual(6) + embed(6, 1),
]
BESIDE = [
    rank(0, 1),
    rank(1, 1),
    rank(2, 1) + rank(3, 0) + rank(3, 1),
    [],
    rank(4, 1) + rank(5, 0) + rank(5, 1),
    [],
    rank(6, 1) + rank(7, 0) + rank(7, 1),
    [],
]
END = residual(7) + embed(7, 1)
SCHEDULE = START + [st for beside, step in zip(BESIDE, STEPS) for st in beside + step] + END

USES = {"pool": [("pool_w", [0])], "latent": [("w_dkv", [0, 1])],
        "keys": [("w_ukv_k", [0]), ("w_ukv_v", [0])], "dq": [("w_dq", [0, 1, 2])],
        "uq": [("w_uq_nope", [0, 1, 2, 3])], "uqp": [("w_uq_pe", [0, 1])], "wo": [("w_o", [0, 1, 2, 3])],
        "asks0": [("wq", [0, 1, 2, 3])], "asks1": [("wq", [4, 5, 6, 7])], "gates": [("ple_wg", [0, 1, 2, 3])],
        "add": [("ple_wp", [0])]}

PARTS = {
    "pool": lambda g, n: [3] + [6, 6] * n + [3],
    "fnorm": lambda g, n: [4] + [4] * n + [2],
    "trig": lambda g, n: [6, 0],
    "asks0": lambda g, n: [5 * n] + [6 * n] * 3 + [4 * n] * 2,
    "asks1": lambda g, n: [5 * n] + [6 * n] * 3 + [3 * n] * 2,
    "rank0": lambda g, n: [10, 10],
    "rank1": lambda g, n: [10, 10],
    "residual": lambda g, n: [2, 0],
    "enorm": lambda g, n: [4] + [4] * n + [2],
    "gates": lambda g, n: [5 * n] * 4 + [2],
    "add": lambda g, n: [5 * n, 4, 1, 1],
    "latent": lambda g, n: [2, 4, 5, 10, 4, 3, 2],
    "keys": lambda g, n: [9, 9, 2],
    "dq": lambda g, n: [9, 9, 9, 2, 4, 4, 2],
    "uq": lambda g, n: [7, 7, 7, 7, 1],
    "uqp": lambda g, n: [7, 7, 5, 3, 3, 1],
    "heads": lambda g, n: [3, 5, 7, 7, 6, 4, 3, 1] if g % NC < 2 else [5, 8, 12, 12, 10, 8, 5, 2],
    "wo": lambda g, n: [9, 9, 9, 9, 2],
}


def incs(stage, g0, n):
    second = 1 if n == 2 else 0
    return {
        "pool": dict(normed=n, t_filled=n, t_copied=n, x_ready=n, pooled=n - 1),
        "fnorm": dict(normed=n, hp_ready=n, t_filled=n, t_copied=n),
        "rank0": dict(idx_ready=1),
        "rank1": dict(idx_ready=1),
        "latent": dict(normed=2 * n, hat_ready=n, t_filled=n + 1, t_copied=n + 1, m_copied=1, b_copied=1),
        "keys": dict(m_copied=2, b_copied=2),
        "dq": dict(normed=n, m_copied=1, b_copied=1, t_filled=n, t_copied=n),
        "uq": dict(m_copied=1, b_copied=1),
        "uqp": dict(m_copied=1, b_copied=1, t_filled=n, t_copied=n),
        "heads": dict(m_copied=2),
        "wo": dict(x_ready=n),
        "residual": dict(x_ready=1),
        "enorm": dict(normed=n, hat_ready=n, t_filled=n, t_copied=n),
        "gates": dict(m_copied=1, b_copied=second),
        "add": dict(m_copied=1, b_copied=second, x_ready=n, normed=n if g0 >= NC else 0),
        "asks0": dict(b_copied=2, m_copied=2, t_filled=4, t_copied=4),
        "asks1": dict(b_copied=2, m_copied=2, t_filled=4, t_copied=4),
    }.get(stage, {})


def totals():
    count, at = {}, {}
    for st in SCHEDULE:
        at[st[:2]] = dict(count)
        for name, n in incs(*st).items():
            count[name] = count.get(name, 0) + n
    return at, count


AT, TOTAL = totals()
EMBED_GROUPS = [g0 for s, g0, n in SCHEDULE if s == "enorm"]
KEY_GROUPS = [g0 for i, (s, g0, n) in enumerate(SCHEDULE) if s == "asks0" and any(
    t in ("pool", "latent") for t, _, _ in SCHEDULE[max([0] + [j for j in range(i) if SCHEDULE[j][0] == "asks0"]):i])]
PLACE = {g0 + i: i for s, g0, n in SCHEDULE if s == "fnorm" for i in range(n)}


def before(name, stage, g0):
    return AT[stage, g0].get(name, 0)


PIECES = {}
for _stage, _g, _n in SCHEDULE:
    for _w, _is in USES.get(_stage, []):
        for _i in _is:
            PIECES[_w, _g, _i] = len(PIECES)


PACE = 6


FIRST_PIECES = sum(len(ids) for st in START for _, ids in USES.get(st[0], []))
FIRST_SLOT = SLOTS - FIRST_PIECES
KEPT = [("wq", (1, 2)), ("ple_wg", (4, 6, 7))]


def homes():
    found, ringed, first = [], [], {}
    for (name, g0, i), n in PIECES.items():
        kept = [(k, groups) for k, (kept_name, groups) in enumerate(KEPT)
                if name == kept_name and g0 in groups and i < 4]
        if n < FIRST_PIECES:
            found.append(("slot", FIRST_SLOT + n, 0, None, False))
        elif kept:
            k, groups = kept[0]
            found.append(("KV", i, k, None, g0 != groups[0]))
        else:
            r = len(ringed)
            found.append(("ring", r % RING, r // RING, ringed[r - RING] if r >= RING else None, False))
            ringed.append(n)
    return found


HOMES = homes()


def placed_parts(g):
    placed, done = [[] for _ in range(UNITS)], 0
    last = UNITS - NB
    total = max(PACE * last, sum(sum(PARTS[st[0]](*st[1:])) for st in STEPS[g]))
    for st in STEPS[g]:
        for part, share in enumerate(PARTS[st[0]](*st[1:])):
            placed[done * last // total].append((st, part))
            done += share
    beside = [(st, part) for st in BESIDE[g] for part in range(len(PARTS[st[0]](*st[1:])))]
    for i, part in enumerate(beside):
        first = 1 + max(u for u in range(UNITS) if any(st[0] == "asks1" for st, _ in placed[u]))
        placed[first + 2 * i if i < 2 else first + 4 + (i - 2) * (last - 1 - first - 4) // 3].append(part)
    return placed


def run_between(stages, gather_batches, open_pair=None, close_pair=None):
    running = {}

    def run_part(st, part):
        stage, g0, n = st
        if stage not in stages:
            return
        if part == 0:
            running[st] = stages[stage](g0, n)
        ended = next(running[st], "ended")
        assert part < len(PARTS[stage](g0, n)) - 1 or ended == "ended", (stage, part)

    def run_all(sts):
        for st in sts:
            for part in range(len(PARTS[st[0]](*st[1:]))):
                run_part(st, part)

    run_all(START)
    for g in range(PAIRS):
        if open_pair:
            open_pair(g)
        placed = placed_parts(g)
        starts = [u for u in range(UNITS) if placed[u] or u == 0]
        for u, end in zip(starts, starts[1:] + [UNITS]):
            for st, part in placed[u]:
                run_part(st, part)
            gather_batches(g, u, end)
        if close_pair:
            close_pair(g)
    run_all(END)


def run_batches(engine, u, end, batch):
    while u < end:
        if u % NB or end - u < NB:
            batch(u // NB, 0, u % NB)
            u += 1
        elif end - u < 2 * NB:
            for b in range(NB):
                batch(u // NB, 0, b)
            u += NB
        else:
            bodies = (end - u) // NB
            with engine.Fori(0, bodies) as it:
                for b in range(NB):
                    batch(u // NB, it, b)
            u += bodies * NB


def trunk(nc, consts, pools, gcols, gains, positions, x, pT, uv, weights, keys, out):
    ctx = ExitStack()
    with ctx:
        def sb(name, shape, dt=F32):
            return ctx.enter_context(nc.sbuf_tensor(name, shape, dt))

        def sem(name):
            return ctx.enter_context(nc.semaphore(name))

        W2 = GROUP * P
        X = sb("X", [P, NC, D])
        KV = sb("KV", [P, 2 * NC * D])
        KT = KV[:, 0:NC * D].rearrange("p (h s) -> p h s", h=H)
        V = KV[:, NC * D:2 * NC * D].rearrange("p (c d) -> p c d", c=NC)
        poolm = KV[:, 0:12 * P].rearrange("p (k w t) -> p k w t", k=3, w=4)
        mix_gain = KV[:, 12 * P:12 * P + D]
        pool_scale = KV[:, 12 * P + D:12 * P + 2 * D]
        hpool = KV[:, 12 * P + 2 * D:12 * P + 4 * D].rearrange("p (i d) -> p i d", i=2)
        KPE = sb("KPE", [ROPE, S])
        cs = sb("cs", [P, 2, NC, HALF])
        cst = sb("cst", [P, C_WIDTH])
        gc = sb("gc", [P, G_WIDTH])
        gain = sb("gain", [P, D])
        HP = sb("HP", [P, HPB, D])
        A = sb("A", [P, 2, D])
        TT = sb("TT", [P, DB, W2])
        TU = sb("TU", [P, DB, W2])
        SC = sb("SC", [P, PIECE])
        SD = sb("SD", [P, PIECE])
        sq_out = sb("sq_out", [P, D], BF16)
        ring = [sb(f"w{i}", [P, PIECE]) for i in range(RING)]
        pt = sb("pt", [P, PLE // P, W2])
        ss = sb("ss", [P, TOTAL["normed"]])
        rms = sb("rms", [P, TOTAL["normed"]])
        rstd = sb("rstd", [P, TOTAL["normed"]])
        slot = [sb(f"slot{i}", [P, 2 * D]) for i in range(SLOTS)]
        places = {"ring": ring, "slot": slot, "KV": [KV[:, i * PIECE:(i + 1) * PIECE] for i in range(4)]}
        diag = {s: sb(f"diag{s}", [P, P]) for s in PE_SLOTS}
        a = sb("a", [P, SLOTS])
        act_a = sb("act_a", [P, SLOTS])
        w = sb("w", [P, SLOTS])
        idx = sb("idx", [P, HPB, KSEL], I32)
        gate = sb("gate", [P, HPB, KSEL])
        top = sb("top", [P, GROUP, PH, 2, TOPK])
        top_u = sb("top_u", [P, GROUP, PH, 2, TOPK], U32)
        top_i = sb("top_i", [P, PH, 2, TOPK])
        best = sb("best", [P, PH, TOPK])
        pos_u = sb("pos_u", [P, PH, TOPK], U32)
        half_f = sb("half_f", [P, 2, KSEL])
        shifted = sb("shifted", [P, PH, TOPK])
        gsum = sb("gsum", [P, PH])
        grec = sb("grec", [P, PH])
        amax = sb("amax", [P, NC * H])
        nmax = sb("nmax", [P, NC * H])
        asum = sb("asum", [P, NC * H])
        arec = sb("arec", [P, NC * H])
        pos_i = sb("pos_i", [P, NC], I32)
        pos_f = sb("pos_f", [P, NC])
        zeros = sb("zeros", [P, P])

        ident = cst[:, C_IDENT:C_IDENT + P]
        mask = cst[:, C_MASK:C_MASK + P]
        iota = cst[:, C_IOTA:C_IOTA + TOPK]
        inv = cst[:, C_INV:C_INV + HALF]
        eps = cst[:, C_EPS:C_EPS + 1]

        def ps(name, width):
            return ctx.enter_context(nc.psum_tensor(name, [P, width], F32))

        acc = ps("acc", D)
        M = ps("M", D)
        T = ps("T", D)
        B = ps("B", D)
        MB = (M, B)
        blocks = "p (b t) -> p b t"

        asked = A[:, :, :].rearrange("p a (q t) -> p a q t", q=4)[:, :, 0:2, :]
        ckv = [SD[:, 320 * i:320 * i + KVR] for i in range(2)]
        kpe = [SD[:, 320 * i + KVR:320 * (i + 1)] for i in range(2)]
        ckvT = SD[:, 640:640 + 2 * W2].rearrange(blocks, b=2)
        qpe = [SD[:, 512 * i:512 * (i + 1)] for i in range(2)]
        rtmp = SD[:, 1536:2048]
        QT = TU
        QPT = A[0:ROPE, :, :].rearrange("p a (b t) -> p (a b) t", t=W2)
        keysT = TU[:, :, :].rearrange("p k (a t) -> p (k a) t", t=P)
        prob = SC[:, :].rearrange("p (k e s) -> p k e s", k=2, e=2)
        probT = SD[:, 0:D].rearrange("p (e s) -> p e s", e=2)
        adiag = SD[:, D:D + 2 * P].rearrange("p (e t) -> p e t", e=2)
        half_u = SC[:, 0:2 * KSEL].bitcast(U32).rearrange("p (i k) -> p i k", i=2)
        outs = [TU[:, 4 * i:4 * i + 4, :].rearrange("p b t -> p (b t)") for i in range(2)] + [SD[:, 0:D], SD[:, D:2 * D]]

        cst_loaded, const_loaded, late_loaded = sem("cst_loaded"), sem("const_loaded"), sem("late_loaded")
        x_loaded = [sem(f"x_loaded{c}") for c in range(NC)]
        w_loaded = {"ring": [sem(f"ring_loaded{i}") for i in range(RING)],
                    "KV": [sem(f"kept_loaded{i}") for i in range(4)],
                    "slot": [sem(f"slot_loaded{i}") for i in range(SLOTS)]}
        keys_loaded = sem("keys_loaded")
        pt_loaded = sem("pt_loaded")
        gain_loaded = sem("gain_loaded")
        weights_used = sem("weights_used")
        normed = sem("normed")
        hat_ready, hp_ready, x_ready = sem("hat_ready"), sem("hp_ready"), sem("x_ready")
        t_filled = sem("t_filled")
        t_copied, m_copied, b_copied = sem("t_copied"), sem("m_copied"), sem("b_copied")
        squared, mixed, pooled = sem("squared"), sem("mixed"), sem("pooled")
        att_scored, att_maxed, att_exped = sem("att_scored"), sem("att_maxed"), sem("att_exped")
        att_normed, att_turned, att_copied, att_out = (sem("att_normed"), sem("att_turned"),
                                                       sem("att_copied"), sem("att_out"))
        gate_shifted, gate_exped = sem("gate_shifted"), sem("gate_exped")
        idx_ready = sem("idx_ready")
        rows_loaded = [sem(f"rows_loaded{i}") for i in range(SLOTS)]
        dotted, gelued, weighted, diag_ready = sem("dotted"), sem("gelued"), sem("weighted"), sem("diag_ready")
        slots_free = sem("slots_free")
        v_added = sem("v_added")
        acc_done = sem("acc_done")
        out_ready, out_stored = sem("out_ready"), sem("out_stored")
        dve_steps = sem("dve_steps")
        trig_shifted, trig_done = sem("trig_shifted"), sem("trig_done")
        zeroed = sem("zeroed")
        copied = (m_copied, b_copied)

        def used(name, g0, i):
            return PIECES[name, g0, i] + 1

        def norm_number(stage, g0, i=0):
            return before("normed", stage, g0) + i

        CONSTS, LATE = 2, 4
        block = ctx.enter_context(nc.Block())

        @block.sync
        def _(sp):
            sp.dma_start(X[:, 0, :], x[0:P, :]).then_inc(x_loaded[0], 16)
            sp.dma_start(cst[:], consts).then_inc(cst_loaded, 16)
            sp.dma_start(mix_gain, gains[0:1, :].broadcast_to([P, D])).then_inc(const_loaded, 16)
            sp.dma_start(KV[:, 0:12 * P], pools).then_inc(const_loaded, 16)
            late_constants = ((pool_scale, gains[1:2, :].broadcast_to([P, D])), (gain[:], gains[2:3, :].broadcast_to([P, D])),
                              (gc[:], gcols), (pos_i[:], positions))
            groups = 0
            for (name, g0, i), n in PIECES.items():
                size = {st[:2]: st[2] for st in SCHEDULE}
                if name == "ple_wp":
                    width, c = size["add", g0] * P, g0 % NC
                    if groups:
                        sp.wait_ge(weights_used, last_wp)
                    sp.dma_start(pt[:, :, 0:width], pT[g0 // NC, :, :, c * P:c * P + width]).then_inc(pt_loaded, 16)
                    groups, last_wp = groups + 1, n + 1
                where, h, loads, had, there = HOMES[n]
                if where == "ring" and had is not None:
                    sp.wait_ge(weights_used, had + 1)
                if where == "KV" and not there and i == 0:
                    next_ffn = NC + 2 if name == "ple_wg" else g0
                    sp.wait_ge(x_ready, before("x_ready", "fnorm", next_ffn))
                if not there:
                    src = weights[name, g0 // NC][i]
                    sp.dma_start(places[where][h][:, 0:src.shape[1]], src).then_inc(w_loaded[where][h], 16)
                if n == 0:
                    for dst, values in late_constants:
                        sp.dma_start(dst, values).then_inc(late_loaded, 16)
                if name == "wq" and i == 1 and g0 in KEY_GROUPS:
                    sp.wait_ge(x_ready, before("x_ready", "fnorm", g0))
                    sp.dma_start(TU[:, :, :], keys[g0 // NC]).then_inc(keys_loaded, 16)
                if n == FIRST_PIECES - 1:
                    for c in range(1, NC):
                        sp.dma_start(X[:, c, :], x[c * P:(c + 1) * P, :]).then_inc(x_loaded[c], 16)
                if (name, i) == ("wq", 7) and g0 in (NC - 2, PAIRS - 2):
                    sp.wait_ge(hp_ready, g0 + 2)
                    sp.dma_start(gain[:], gains[3 + g0 // NC:4 + g0 // NC, :].broadcast_to([P, D])
                                 ).then_inc(gain_loaded, 16)

        @block.gpsimd
        def _(pool):
            for g in range(PAIRS):
                for k in range(KSEL):
                    if k % (KSEL // 2) == 0:
                        half = k // (KSEL // 2)
                        pool.wait_ge(idx_ready, before("idx_ready", f"rank{half}", g) + 1)
                    body, s = (g * KSEL + k) // SLOTS, k % SLOTS
                    if body == 0 and s >= FIRST_SLOT:
                        pool.wait_ge(weights_used, s - FIRST_SLOT + 1)
                    if s in DVE_SLOTS:
                        pool.wait_ge(v_added, body * NDVE + DVE_SLOTS.index(s) + 1)
                    else:
                        pool.wait_ge(slots_free, body * NPE + PE_SLOTS.index(s) + 1)
                    nc.gpsimd.indirect_dma_start(
                        out=slot[s][:], out_offset=None, in_=uv[g // NC],
                        in_offset=bass.IndirectOffsetOnAxis(ap=idx[:, g % HPB, k:k + 1], axis=0),
                    ).then_inc(rows_loaded[s], 16)

        @block.tensor
        def _(pe):
            def piece(name, g0, i):
                where, h, loads, _, _ = HOMES[PIECES[name, g0, i]]
                pe.wait_ge(w_loaded[where][h], 16 * (loads + 1))
                return places[where][h]

            def transposes(src, n, width=P, at=0):
                for b in range(n):
                    last = nc.tensor.transpose(T[0:width, at + b * P:at + (b + 1) * P],
                                               src[:, b * width:(b + 1) * width], ident)
                return last

            def product(dst, lhsT, i, wp, kb, cols):
                for k in range(kb):
                    last = nc.tensor.matmul(dst, lhsT[:, k, i * P:(i + 1) * P], wp[:, k * cols:(k + 1) * cols],
                                            start=(k == 0), stop=(k == kb - 1))
                return last

            def products(g0, n, name, pieces, lhsT, kb, cols, at=lambda i: i * 256):
                for i in pieces:
                    wp = piece(name, g0, i)
                    for ch in range(n):
                        last = product(MB[ch][:, at(i):at(i) + cols], lhsT, ch, wp, kb, cols)
                    last.then_inc(weights_used, 1)

            def wait_mb(stage, g0, n=2):
                for ch, name in list(enumerate(("m_copied", "b_copied")))[:n]:
                    if before(name, stage, g0):
                        pe.wait_ge(copied[ch], before(name, stage, g0))

            def pool_stage(g0, n):
                for i in range(n):
                    yield
                    g = g0 + i
                    pe.wait_ge(mixed, g + 1)
                    if g:
                        pe.wait_ge(t_copied, before("t_copied", "pool", g0) + i)
                    for b in range(DB):
                        wnd = b // 2
                        dst = T[:, b * P:(b + 1) * P]
                        if g:
                            nc.tensor.matmul(dst, hpool[:, (g - 1) % 2, b * P:(b + 1) * P], poolm[:, 2, wnd, :],
                                             start=True, stop=False)
                        last = nc.tensor.matmul(dst, hpool[:, g % 2, b * P:(b + 1) * P],
                                                poolm[:, 1 if g else 0, wnd, :], start=(g == 0), stop=True)
                    last.then_inc(t_filled, 1)
                    yield
                    pe.wait_ge(t_copied, before("t_copied", "pool", g0) + i + 1)
                    if i:
                        pe.wait_ge(x_ready, before("x_ready", "pool", g0) + i)
                    else:
                        wait_mb("pool", g0, 1)
                        wp = piece("pool_w", g0, 0)
                    for wnd in range(len(WINDOWS)):
                        for k in range(2):
                            last = nc.tensor.matmul(M[:, wnd * GW:(wnd + 1) * GW], TU[:, 2 * wnd + k, 0:P],
                                                    wp[:, (2 * wnd + k) * GW:(2 * wnd + k + 1) * GW],
                                                    start=(k == 0), stop=(k == 1))
                    last.then_inc(pooled if i < n - 1 else weights_used, 1)

            def fnorm_stage(g0, n):
                for i in range(n):
                    yield
                    pe.wait_ge(hp_ready, g0 + i + 1)
                    pe.wait_ge(t_copied, before("t_copied", "fnorm", g0) + i)
                    transposes(HP[:, (g0 + i) % HPB, :], DB).then_inc(t_filled, 1)

            def asks_stage(half, g0, n):
                stage, width = f"asks{half}", n * P

                def queries(p):
                    dst, name = ((B, "b_copied"), (M, "m_copied"))[p % 2]
                    if before(name, stage, g0) + p // 2:
                        pe.wait_ge((b_copied, m_copied)[p % 2], before(name, stage, g0) + p // 2)
                    if p == 0:
                        pe.wait_ge(t_copied, before("t_copied", stage, g0))
                    wp = piece("wq", g0, 4 * half + p)
                    for e in range(2):
                        for k in range(DB):
                            last = nc.tensor.matmul(dst[:, e * 512:e * 512 + width],
                                                    wp[:, k * 256 + e * P:k * 256 + (e + 1) * P],
                                                    TT[:, k, 0:width], start=(k == 0), stop=(k == DB - 1))
                    last.then_inc(weights_used, 1)

                def scores(p):
                    if p == 0:
                        pe.wait_ge(keys_loaded, 16 * sum(g <= g0 for g in KEY_GROUPS))
                    name = ("b_copied", "m_copied")[p % 2]
                    pe.wait_ge((b_copied, m_copied)[p % 2], before(name, stage, g0) + p // 2 + 1)
                    if p >= 2:
                        pe.wait_ge(t_copied, before("t_copied", stage, g0) + p - 1)
                    for i in range(n):
                        for e in range(2):
                            at = (p % 2) * 512 + (2 * i + e) * P
                            last = nc.tensor.matmul(T[:, at:at + P], asked[:, p % 2, e, i * P:(i + 1) * P],
                                                    keysT[:, 8 * half + 2 * p + e, :], start=True, stop=True)
                    last.then_inc(t_filled, 1)

                for p in range(4):
                    queries(p)
                    if p:
                        scores(p - 1)
                    yield
                scores(3)

            def latent_stage(g0, n):
                t0 = before("t_copied", "latent", g0)
                for i in range(n):
                    yield
                    pe.wait_ge(hat_ready, before("hat_ready", "latent", g0) + i + 1)
                    pe.wait_ge(t_copied, t0 + i)
                    transposes(A[:, i, :], DB).then_inc(t_filled, 1)
                yield
                pe.wait_ge(t_copied, t0 + n)
                wait_mb("latent", g0)
                products(g0, n, "w_dkv", [0], TU, DB, KVR, lambda i: 0)
                products(g0, n, "w_dkv", [1], TU, DB, ROPE, lambda i: 512)
                yield
                yield
                for i in range(n):
                    pe.wait_ge(copied[i], before(("m_copied", "b_copied")[i], "latent", g0) + 1)
                    transposes(ckv[i], 2, at=512 * i)
                    last = nc.tensor.transpose(T[0:ROPE, 512 * i + KVR:512 * i + KVR + P], kpe[i], ident)
                last.then_inc(t_filled, 1)

            def keys_stage(g0, n):
                pe.wait_ge(t_copied, before("t_copied", "keys", g0))
                wait_mb("keys", g0)
                wp = piece("w_ukv_k", g0, 0)
                for h in range(H):
                    for k in range(2):
                        last = nc.tensor.matmul(MB[h // 4][:, (h % 4) * W2:(h % 4 + 1) * W2],
                                                wp[:, k * 1024 + h * P:k * 1024 + (h + 1) * P],
                                                ckvT[:, k, :], start=(k == 0), stop=(k == 1))
                last.then_inc(weights_used, 1)
                yield
                wp = piece("w_ukv_v", g0, 0)
                for i in range(n):
                    pe.wait_ge(copied[i], before(("m_copied", "b_copied")[i], "keys", g0) + 1)
                    for half in range(2):
                        last = product(MB[i][:, half * 512:half * 512 + 512], ckvT, i,
                                       wp[:, half * 1024:half * 1024 + 1024], 2, 512)
                last.then_inc(weights_used, 1)

            def dq_stage(g0, n):
                wait_mb("dq", g0)
                for i in range(3):
                    products(g0, n, "w_dq", [i], TT, DB, 256)
                    yield
                for i in range(n):
                    yield
                    pe.wait_ge(copied[i], before(("m_copied", "b_copied")[i], "dq", g0) + 1)
                    pe.wait_ge(t_copied, before("t_copied", "dq", g0) + i)
                    transposes(A[:, i, :], QR // P).then_inc(t_filled, 1)

            def uq_stage(g0, n):
                pe.wait_ge(t_copied, before("t_copied", "uq", g0))
                wait_mb("uq", g0)
                for q in range(4):
                    wp = piece("w_uq_nope", g0, q)
                    for e in range(2):
                        at = (2 * (q % 2) + e) * W2
                        for k in range(QR // P):
                            last = nc.tensor.matmul(MB[q // 2][:, at:at + W2],
                                                    wp[:, k * 256 + e * P:k * 256 + (e + 1) * P], TT[:, k, :],
                                                    start=(k == 0), stop=(k == QR // P - 1))
                    last.then_inc(weights_used, 1)
                    yield

            def uqp_stage(g0, n):
                wait_mb("uqp", g0)
                for i in range(2):
                    products(g0, n, "w_uq_pe", [i], TT, QR // P, 256)
                    yield
                for i in range(n):
                    yield
                    pe.wait_ge(copied[i], before(("m_copied", "b_copied")[i], "uqp", g0) + 1)
                    pe.wait_ge(t_copied, before("t_copied", "uqp", g0) + i)
                    transposes(qpe[i], H, ROPE).then_inc(t_filled, 1)

            def heads_stage(g, n):
                c = g % NC
                width = (c + 1) * P
                q0 = (g % GROUP) * P
                pair0 = c * HEAD_PAIRS

                def score(k):
                    if k == 0:
                        pe.wait_ge(b_copied, before("b_copied", "heads", g))
                        pe.wait_ge(t_copied, before("t_copied", "heads", g))
                    if pair0 + k:
                        pe.wait_ge(att_exped, 2 * (pair0 + k))
                    for e in range(2):
                        dst, h = B[:, e * 512:e * 512 + width], 2 * k + e
                        nc.tensor.matmul(dst, QT[:, h, q0:q0 + P], KT[:, h, 0:width], start=True, stop=False)
                        last = nc.tensor.matmul(dst, QPT[:, h, q0:q0 + P], KPE[:, 0:width], start=False, stop=True)
                    last.then_inc(att_scored, 1)

                def turn(k):
                    pe.wait_ge(att_normed, pair0 + k + 1)
                    if pair0 + k:
                        pe.wait_ge(att_copied, pair0 + k)
                    for e in range(2):
                        for b in range(c + 1):
                            last = nc.tensor.matmul(T[:, e * 512 + b * P:e * 512 + (b + 1) * P],
                                                    prob[:, k % 2, e, b * P:(b + 1) * P], adiag[:, e, :],
                                                    start=True, stop=True)
                    last.then_inc(att_turned, 1)

                def output(k):
                    pe.wait_ge(att_copied, pair0 + k + 1)
                    if k == 0:
                        pe.wait_ge(m_copied, before("m_copied", "heads", g))
                    for e in range(2):
                        h = 2 * k + e
                        for b in range(c + 1):
                            last = nc.tensor.matmul(M[:, h * P:(h + 1) * P], V[:, b, h * P:(h + 1) * P],
                                                    probT[:, e, b * P:(b + 1) * P], start=(b == 0), stop=(b == c))
                    last.then_inc(att_out, 1)

                for part in range(HEAD_PAIRS + 3):
                    if part >= 3:
                        output(part - 3)
                    if 2 <= part < HEAD_PAIRS + 2:
                        turn(part - 2)
                    if part < HEAD_PAIRS:
                        score(part)
                    yield

            def wo_stage(g0, n):
                wait_mb("wo", g0)
                for i in range(4):
                    products(g0, n, "w_o", [i], TT, DB, 256)
                    yield

            def enorm_stage(g0, n):
                for i in range(n):
                    yield
                    pe.wait_ge(hat_ready, before("hat_ready", "enorm", g0) + i + 1)
                    pe.wait_ge(t_copied, before("t_copied", "enorm", g0) + i)
                    transposes(A[:, i, :], DB).then_inc(t_filled, 1)

            def gates_stage(g0, n):
                pe.wait_ge(t_copied, before("t_copied", "gates", g0))
                wait_mb("gates", g0, n)
                for i in range(4):
                    products(g0, n, "ple_wg", [i], TT, DB, 256)
                    yield

            def add_stage(g0, n):
                pe.wait_ge(pt_loaded, 16 * (EMBED_GROUPS.index(g0) + 1))
                wait_mb("add", g0, n)
                wp = piece("ple_wp", g0, 0)
                for i in range(n):
                    for half in range(2):
                        last = product(MB[i][:, half * 512:half * 512 + 512], pt, i,
                                       wp[:, half * 1024:half * 1024 + 1024], 2, 512)
                last.then_inc(weights_used, 1)
                yield

            stages = dict(pool=pool_stage, fnorm=fnorm_stage, asks0=lambda g, n: asks_stage(0, g, n),
                          asks1=lambda g, n: asks_stage(1, g, n), latent=latent_stage, keys=keys_stage,
                          dq=dq_stage, uq=uq_stage, uqp=uqp_stage, heads=heads_stage, wo=wo_stage,
                          enorm=enorm_stage, gates=gates_stage, add=add_stage)

            def zero_sums(g, start, stop):
                for half in range(2):
                    last = nc.tensor.matmul(acc[:, half * 512:half * 512 + 512], zeros[:], HP[:, g % HPB, 0:512],
                                            start=start, stop=stop)
                return last

            def open_pair(g):
                if g == 0:
                    zero_sums(g, True, False).then_inc(slots_free, NPE)

            def reopen(g):
                pe.wait_ge(x_ready, before("x_ready", "residual", g - 1) + 1)
                zero_sums(g, True, False)

            def gather_batches(g, u, end):
                if g and u == 0:
                    reopen(g)

                def batch(j, it, b):
                    first = g * BODIES + j
                    for p, s in enumerate(PE_SLOTS):
                        if s // BATCH != b:
                            continue
                        pe.wait_ge(diag_ready, it * NPE + (first * NPE + p + 1))
                        for half in range(2):
                            last = nc.tensor.matmul(acc[:, half * 512:half * 512 + 512], diag[s][:],
                                                    slot[s][:, D + half * 512:D + half * 512 + 512],
                                                    start=False, stop=False)
                        last.then_inc(slots_free, 1)

                run_batches(pe, u, end, batch)

            def close_pair(g):
                zero_sums(g, False, True).then_inc(acc_done, 1)

            pe.wait_ge(cst_loaded, 16)
            pe.wait_ge(const_loaded, 16 * CONSTS)
            pe.wait_ge(zeroed, 1)
            run_between(stages, gather_batches, open_pair, close_pair)

        @block.scalar
        def _(act):
            def norm(stage, g0, src, width, i=0):
                n = norm_number(stage, g0, i)
                nc.scalar.activation(sq_out[:, 0:width], src, ACT.Square, accum_out=ss[:, n:n + 1]
                                     ).then_inc(squared, 1)
                act.wait_ge(squared, n + 1)
                nc.scalar.activation(rms[:, n:n + 1], ss[:, n:n + 1], ACT.Sqrt, bias=eps, scale=1.0 / width
                                     ).then_inc(normed, 1)

            def pool_stage(g0, n):
                for i in range(n):
                    act.wait_ge(x_loaded[g0 + i], 16)
                    norm("pool", g0, X[:, g0 + i, :], D, i)
                for i in range(n):
                    yield
                    yield
                    act.wait_ge(t_filled, before("t_filled", "pool", g0) + i + 1)
                    if i:
                        act.wait_ge(pooled, before("pooled", "pool", g0) + i)
                    nc.scalar.activation(TU[:, :, 0:P], T[:, :].rearrange(blocks, t=P), ACT.Copy).then_inc(t_copied, 1)

            def fnorm_stage(g0, n):
                act.wait_ge(x_ready, before("x_ready", "fnorm", g0))
                for i in range(n):
                    norm("fnorm", g0, X[:, (g0 + i) % NC, :], D, i)
                yield
                for i in range(n):
                    yield
                    act.wait_ge(t_filled, before("t_filled", "fnorm", g0) + i + 1)
                    nc.scalar.activation(TT[:, :, i * P:(i + 1) * P], T[:, :].rearrange(blocks, t=P), ACT.Copy
                                         ).then_inc(t_copied, 1)

            def asks_stage(half, g0, n):
                stage = f"asks{half}"
                for p in range(4):
                    yield
                    act.wait_ge(weights_used, used("wq", g0, 4 * half + p))
                    if p >= 2:
                        act.wait_ge(t_filled, before("t_filled", stage, g0) + p - 1)
                    nc.scalar.activation(asked[:, p % 2, :, 0:n * P],
                                         (B, M)[p % 2][:, :].rearrange("p (e t) -> p e t", e=2)[:, :, 0:n * P],
                                         ACT.Copy).then_inc((b_copied, m_copied)[p % 2], 1)

            def trig_stage(g, n):
                yield
                act.wait_ge(trig_shifted, 1)
                nc.scalar.activation(cs[:, :, :, :], cs[:, :, :, :], ACT.Sin).then_inc(trig_done, 1)

            def rank_stage(half, g, n):
                yield
                turn = before("idx_ready", f"rank{half}", g) + 1
                act.wait_ge(gate_shifted, turn)
                hs = slice(4 * half, 4 * half + 4)
                nc.scalar.activation(shifted[:, hs, :], shifted[:, hs, :], ACT.Exp).then_inc(gate_exped, 1)

            def latent_stage(g0, n):
                act.wait_ge(x_ready, before("x_ready", "latent", g0))
                for i in range(n):
                    norm("latent", g0, X[:, (g0 + i) % NC, :], D, i)
                for _ in range(4):
                    yield
                act.wait_ge(weights_used, used("w_dkv", g0, 0))
                for i in range(n):
                    norm("latent", g0, MB[i][:, 0:KVR], KVR, n + i)

            def keys_stage(g0, n):
                c = g0 % NC
                yield
                act.wait_ge(weights_used, used("w_ukv_k", g0, 0))
                for i in range(2):
                    nc.scalar.activation(KT[:, 4 * i:4 * i + 4, c * P:(c + 2) * P], MB[i][:, :].rearrange(blocks, t=W2),
                                         ACT.Copy).then_inc(copied[i], 1)
                yield
                act.wait_ge(weights_used, used("w_ukv_v", g0, 0))
                for i in range(n):
                    nc.scalar.activation(V[:, c + i, :], MB[i][:, :], ACT.Copy).then_inc(copied[i], 1)

            def dq_stage(g0, n):
                for _ in range(3):
                    yield
                act.wait_ge(weights_used, used("w_dq", g0, 2))
                for i in range(n):
                    norm("dq", g0, MB[i][:, 0:QR], QR, i)

            def uq_stage(g0, n):
                for half in range(2):
                    yield
                    yield
                    act.wait_ge(weights_used, used("w_uq_nope", g0, 2 * half + 1))
                    nc.scalar.activation(QT[:, 4 * half:4 * half + 4, :], MB[half][:, :].rearrange(blocks, t=W2),
                                         ACT.Copy).then_inc(copied[half], 1)

            def uqp_stage(g0, n):
                for _ in range(3):
                    yield
                for i in range(n):
                    yield
                    act.wait_ge(t_filled, before("t_filled", "uqp", g0) + i + 1)
                    nc.scalar.activation(QPT[:, :, i * P:(i + 1) * P], T[0:ROPE, :].rearrange(blocks, t=P), ACT.Copy
                                         ).then_inc(t_copied, 1)

            def heads_stage(g, n):
                c = g % NC
                width = (c + 1) * P
                pair0 = c * HEAD_PAIRS
                at = (g % GROUP) * P

                def copy(k):
                    act.wait_ge(att_turned, pair0 + k + 1)
                    if pair0 + k:
                        act.wait_ge(att_out, pair0 + k)
                    nc.scalar.activation(probT[:, :, 0:width], T[:, :].rearrange("p (e s) -> p e s", e=2)[:, :, 0:width],
                                         ACT.Copy).then_inc(att_copied, 1)

                def exp(k):
                    act.wait_ge(att_maxed, pair0 + k + 1)
                    for e in range(2):
                        n = c * H + 2 * k + e
                        nc.scalar.activation(prob[:, k % 2, e, 0:width], B[:, e * 512:e * 512 + width], ACT.Exp,
                                             bias=nmax[:, n:n + 1], scale=SCALE, accum_out=asum[:, n:n + 1]
                                             ).then_inc(att_exped, 1)

                for part in range(HEAD_PAIRS + 4):
                    if 3 <= part < HEAD_PAIRS + 3:
                        copy(part - 3)
                    if 1 <= part < HEAD_PAIRS + 1:
                        exp(part - 1)
                    if part >= 5 and part % 2:
                        half = (part - 5) // 2
                        act.wait_ge(att_out, pair0 + 2 * half + 2)
                        nc.scalar.activation(TT[:, 4 * half:4 * half + 4, at:at + P],
                                             M[:, half * 512:half * 512 + 512].rearrange(blocks, t=P), ACT.Copy
                                             ).then_inc(m_copied, 1)
                    if part < HEAD_PAIRS + 3:
                        yield

            def enorm_stage(g0, n):
                act.wait_ge(x_ready, before("x_ready", "enorm", g0))
                for i in range(n):
                    norm("enorm", g0, X[:, (g0 + i) % NC, :], D, i)
                yield

            def gates_stage(g0, n):
                for _ in range(4):
                    yield
                act.wait_ge(weights_used, used("ple_wg", g0, 3))
                for i in range(n):
                    nc.scalar.activation(A[:, i, :], MB[i][:, :], ACT.Sigmoid).then_inc(copied[i], 1)

            def add_stage(g0, n):
                yield
                yield
                if g0 >= NC:
                    for i in range(n):
                        act.wait_ge(x_ready, before("x_ready", "add", g0) + i + 1)
                        norm("add", g0, X[:, (g0 + i) % NC, :], D, i)
                    yield
                    for i in range(n):
                        c = (g0 + i) % NC
                        act.wait_ge(out_ready, c + 1)
                        act.dma_start(out[c * P:(c + 1) * P, :], outs[c]).then_inc(out_stored, 16)

            stages = dict(pool=pool_stage, fnorm=fnorm_stage, asks0=lambda g, n: asks_stage(0, g, n),
                          asks1=lambda g, n: asks_stage(1, g, n), trig=trig_stage,
                          rank0=lambda g, n: rank_stage(0, g, n), rank1=lambda g, n: rank_stage(1, g, n),
                          latent=latent_stage, keys=keys_stage, dq=dq_stage, uq=uq_stage, uqp=uqp_stage,
                          heads=heads_stage, enorm=enorm_stage, gates=gates_stage, add=add_stage)

            def gather_batches(g, u, end):
                def batch(j, it, b):
                    first = g * BODIES + j
                    at = slice(b * BATCH, (b + 1) * BATCH)
                    act.wait_ge(dotted, it * SLOTS + (first * SLOTS + (b + 1) * BATCH))
                    nc.scalar.activation(act_a[:, at], a[:, at], ACT.Gelu_apprx_tanh).then_inc(gelued, 1)
                    act.wait_ge(weighted, it * NB + (first * NB + b + 1))
                    for p, s in enumerate(PE_SLOTS):
                        if s // BATCH == b:
                            act.wait_ge(slots_free, it * NPE + (first * NPE + p + 1))
                            nc.scalar.activation(diag[s][:], ident, ACT.Copy, scale=w[:, s:s + 1]
                                                 ).then_inc(diag_ready, 1)

                run_batches(act, u, end, batch)

            act.wait_ge(cst_loaded, 16)
            run_between(stages, gather_batches)
            act.wait_ge(out_stored, 16 * NC)

        @block.vector
        def _(dve):
            steps = [0]

            def step(ins):
                ins.then_inc(dve_steps, 1)
                steps[0] += 1

            def settle():
                dve.wait_ge(dve_steps, steps[0])

            def reciprocal_rms(stage, g0, i=0):
                n = norm_number(stage, g0, i)
                dve.wait_ge(normed, n + 1)
                step(nc.vector.reciprocal(rstd[:, n:n + 1], rms[:, n:n + 1]))
                settle()
                return rstd[:, n:n + 1]

            def columns(at, n):
                return gc[:, at:at + n].unsqueeze(2).broadcast_to([P, n, P])

            def pool_stage(g0, n):
                def mix(i):
                    g = g0 + i
                    r = reciprocal_rms("pool", g0, i)
                    if g >= 2:
                        dve.wait_ge(t_filled, before("t_filled", "pool", g0) + i)
                    nc.vector.scalar_tensor_tensor(hpool[:, g % 2, :], X[:, g, :], r, mix_gain, ALU.mult, ALU.mult
                                                   ).then_inc(mixed, 1)

                def add(i):
                    g = g0 + i
                    if g == 0:
                        dve.wait_ge(late_loaded, 16 * LATE)
                    if i < n - 1:
                        dve.wait_ge(pooled, before("pooled", "pool", g0) + i + 1)
                    else:
                        dve.wait_ge(weights_used, used("pool_w", g0, 0))
                    step(nc.vector.tensor_tensor(SD[:, 0:D], M[:, :], pool_scale, ALU.mult))
                    settle()
                    nc.vector.tensor_tensor(X[:, g, :], X[:, g, :], SD[:, 0:D], ALU.add).then_inc(x_ready, 1)

                mix(0)
                for i in range(n):
                    yield
                    if i:
                        add(i - 1)
                    yield
                    if i < n - 1:
                        mix(i + 1)
                yield
                add(n - 1)

            def fnorm_stage(g0, n):
                yield
                for i in range(n):
                    g = g0 + i
                    r = reciprocal_rms("fnorm", g0, i)
                    if g == NC:
                        dve.wait_ge(gain_loaded, 16)
                    nc.vector.scalar_tensor_tensor(HP[:, g % HPB, :], X[:, g % NC, :], r, gain[:, :], ALU.mult, ALU.mult
                                                   ).then_inc(hp_ready, 1)

            def top16(n, values, left, tops, places):
                for i in range(n):
                    step(nc.vector.max(tops(i)[:, 0:8], values(i)))
                settle()
                for i in range(n):
                    step(nc.vector.match_replace(left(i), tops(i)[:, 0:8], values(i), LOW))
                    step(nc.vector.max_index(places(i)[:, 0:8], tops(i)[:, 0:8], values(i)))
                settle()
                for i in range(n):
                    step(nc.vector.max(tops(i)[:, 8:16], left(i)))
                settle()
                for i in range(n):
                    last = nc.vector.max_index(places(i)[:, 8:16], tops(i)[:, 8:16], left(i))
                    if i < n - 1:
                        step(last)
                return last

            def asks_stage(half, g0, n):
                stage = f"asks{half}"
                yield
                for p in range(4):
                    yield
                    dve.wait_ge(t_filled, before("t_filled", stage, g0) + p + 1)
                    j = p % 2
                    top16(2 * n, lambda r: T[:, j * 512 + r * P:j * 512 + (r + 1) * P],
                          lambda r: SD[:, j * D + r * P:j * D + (r + 1) * P],
                          lambda r: top[:, r // 2, 4 * half + p, r % 2, :],
                          lambda r: top_u[:, r // 2, 4 * half + p, r % 2, :]).then_inc(t_copied, 1)

            def rank_stage(half, g, n):
                i, hs, nh = PLACE[g], slice(4 * half, 4 * half + 4), 4
                asks = f"asks{half}", g - i
                turn = before("idx_ready", f"rank{half}", g) + 1
                dve.wait_ge(t_copied, before("t_copied", *asks) + 4)
                step(nc.vector.tensor_copy(top_i[:, hs, :, :], top_u[:, i, hs, :, :]))
                n2 = TOPK * TOPK
                cand = SC[:, 0:nh * n2].rearrange("p (h i j) -> p h i j", h=nh, i=TOPK)
                step(nc.vector.tensor_tensor(
                    cand, top[:, i, hs, 0, :].unsqueeze(3).broadcast_to([P, nh, TOPK, TOPK]),
                    top[:, i, hs, 1, :].unsqueeze(2).broadcast_to([P, nh, TOPK, TOPK]), ALU.add))
                settle()
                step(top16(nh, lambda h: SC[:, h * n2:(h + 1) * n2], lambda h: SC[:, D + h * n2:D + (h + 1) * n2],
                           lambda h: best[:, 4 * half + h, :], lambda h: pos_u[:, 4 * half + h, :]))
                settle()
                nc.vector.tensor_tensor(shifted[:, hs, :], best[:, hs, :], best[:, hs, 0:1].broadcast_to([P, nh, TOPK]),
                                        ALU.subtract).then_inc(gate_shifted, 1)
                yield
                nk = nh * TOPK
                flat = pos_u[:, hs, :].rearrange("p h k -> p (h k)")
                step(nc.vector.tensor_scalar(half_u[:, 0, 0:nk], flat, 4, None, ALU.logical_shift_right))
                step(nc.vector.tensor_scalar(half_u[:, 1, 0:nk], flat, TOPK - 1, None, ALU.bitwise_and))
                settle()
                step(nc.vector.tensor_copy(half_f[:, :, 0:nk], half_u[:, :, 0:nk]))
                settle()
                onehot = [SC[:, p * D:(p + 1) * D] for p in range(2)]
                for p in range(2):
                    step(nc.vector.tensor_tensor(
                        onehot[p].rearrange("p (n j) -> p n j", j=TOPK),
                        half_f[:, p, 0:nk].unsqueeze(2).broadcast_to([P, nk, TOPK]),
                        iota.unsqueeze(1).broadcast_to([P, nk, TOPK]), ALU.is_equal))
                settle()
                for p in range(2):
                    v = onehot[p].rearrange("p (h k j) -> p h k j", h=nh, k=TOPK)
                    step(nc.vector.tensor_tensor(
                        v, v, top_i[:, hs, p, :].unsqueeze(2).broadcast_to([P, nh, TOPK, TOPK]), ALU.mult))
                settle()
                for p in range(2):
                    step(nc.vector.reduce_sum(half_f[:, p, 0:nk], onehot[p].rearrange("p (n j) -> p n j", j=TOPK),
                                              axis=AX))
                settle()
                ks = slice(half * nk, (half + 1) * nk)
                nc.vector.scalar_tensor_tensor(idx[:, g % HPB, ks], half_f[:, 0, 0:nk], float(P), half_f[:, 1, 0:nk],
                                               ALU.mult, ALU.add).then_inc(idx_ready, 1)
                dve.wait_ge(gate_exped, turn)
                step(nc.vector.reduce_sum(gsum[:, hs], shifted[:, hs, :], axis=AX))
                settle()
                step(nc.vector.reciprocal(grec[:, hs], gsum[:, hs]))
                settle()
                step(nc.vector.tensor_tensor(gate[:, g % HPB, ks].rearrange("p (h k) -> p h k", h=nh), shifted[:, hs, :],
                                             grec[:, hs].unsqueeze(2).broadcast_to([P, nh, TOPK]), ALU.mult))
                settle()

            def trig_stage(g, n):
                step(nc.vector.tensor_copy(pos_f[:], pos_i[:]))
                settle()
                angle, turns = SC[:, 0:NC * HALF], SC[:, 512:512 + NC * HALF]
                magic = float(np.float32(1.5 * 2 ** 23))
                part1 = 6.28125
                part2 = float(np.float32(np.float32(0.0019350051879882812)))
                part3 = float(np.float32(2 * np.pi - part1 - part2))
                for c in range(NC):
                    step(nc.vector.tensor_scalar(angle[:, c * HALF:(c + 1) * HALF], inv, pos_f[:, c:c + 1], None, ALU.mult))
                settle()
                for i, ahead in ((0, 0.25), (1, 0.0)):
                    dst = cs[:, i, :, :].rearrange("p c d -> p (c d)")
                    step(nc.vector.tensor_scalar(turns, angle, float(1 / (2 * np.pi)), ahead, ALU.mult, ALU.add))
                    settle()
                    step(nc.vector.tensor_scalar(turns, turns, magic, None, ALU.add))
                    settle()
                    step(nc.vector.tensor_scalar(turns, turns, -magic, None, ALU.add))
                    settle()
                    step(nc.vector.scalar_tensor_tensor(dst, turns, -part1, angle, ALU.mult, ALU.add))
                    settle()
                    step(nc.vector.scalar_tensor_tensor(dst, turns, -part2, dst, ALU.mult, ALU.add))
                    settle()
                    step(nc.vector.scalar_tensor_tensor(dst, turns, -part3, dst, ALU.mult, ALU.add))
                    settle()
                    step(nc.vector.tensor_scalar(dst, dst, float(np.pi / 2) if ahead else 0.0, float(np.float32(3.1415925)),
                                                 ALU.add, ALU.min))
                    settle()
                    last = nc.vector.tensor_scalar(dst, dst, -float(np.float32(3.1415925)), None, ALU.max)
                    if i == 0:
                        step(last)
                        settle()
                last.then_inc(trig_shifted, 1)
                yield

            def rope(dst, src, heads, c, tmp):
                def bc(i):
                    return cs[:, i, c, :].unsqueeze(1).broadcast_to([P, heads, HALF])
                s3 = src.rearrange("p (h d) -> p h d", h=heads)
                d3 = dst.rearrange("p (h d) -> p h d", h=heads)
                n = heads * HALF
                t3 = tmp[:, 0:n].rearrange("p (h d) -> p h d", h=heads)
                u3 = tmp[:, 256:256 + n].rearrange("p (h d) -> p h d", h=heads)
                lo, hi = slice(0, HALF), slice(HALF, ROPE)
                step(nc.vector.tensor_tensor(d3[:, :, lo], s3[:, :, lo], bc(0), ALU.mult))
                step(nc.vector.tensor_tensor(t3, s3[:, :, hi], bc(1), ALU.mult))
                step(nc.vector.tensor_tensor(d3[:, :, hi], s3[:, :, hi], bc(0), ALU.mult))
                step(nc.vector.tensor_tensor(u3, s3[:, :, lo], bc(1), ALU.mult))
                settle()
                step(nc.vector.tensor_tensor(d3[:, :, lo], d3[:, :, lo], t3, ALU.subtract))
                return nc.vector.tensor_tensor(d3[:, :, hi], d3[:, :, hi], u3, ALU.add)

            def latent_stage(g0, n):
                c, t0 = g0 % NC, before("t_filled", "latent", g0)
                yield
                for i in range(n):
                    r = reciprocal_rms("latent", g0, i)
                    nc.vector.tensor_scalar(A[:, i, :], X[:, c + i, :], r, None, ALU.mult).then_inc(hat_ready, 1)
                for i in range(n):
                    yield
                    dve.wait_ge(t_filled, t0 + i + 1)
                    at = slice(i * P, (i + 1) * P)
                    tv = T[:, :].rearrange(blocks, t=P)
                    nc.vector.tensor_tensor(TU[:, :, at], tv, columns(G_KV, DB), ALU.mult)
                    nc.vector.tensor_tensor(TT[:, :, at], tv, columns(G_MIX1, DB), ALU.mult).then_inc(t_copied, 1)
                yield
                dve.wait_ge(weights_used, used("w_dkv", g0, 1))
                if g0 == NC:
                    dve.wait_ge(trig_done, 1)
                for i in range(n):
                    step(rope(kpe[i], MB[i][:, 512:512 + ROPE], 1, c + i, rtmp))
                    settle()
                yield
                for i in range(n):
                    r = reciprocal_rms("latent", g0, n + i)
                    nc.vector.tensor_scalar(ckv[i], MB[i][:, 0:KVR], r, None, ALU.mult).then_inc(copied[i], 1)
                yield
                dve.wait_ge(t_filled, t0 + n + 1)
                ti = T[:, :].rearrange("p (i b t) -> p i b t", i=2, b=4)
                nc.vector.tensor_tensor(
                    ckvT.rearrange("p b (i t) -> p i b t", i=2), ti[:, :, 0:2, :],
                    gc[:, G_CKV:G_CKV + 2].unsqueeze(1).unsqueeze(3).broadcast_to([P, 2, 2, P]), ALU.mult)
                nc.vector.tensor_copy(KPE[:, c * P:(c + 2) * P].rearrange("p (i t) -> p i t", i=2), ti[0:ROPE, :, 2, :]
                                      ).then_inc(t_copied, 1)

            def dq_stage(g0, n):
                for _ in range(4):
                    yield
                for i in range(n):
                    r = reciprocal_rms("dq", g0, i)
                    nc.vector.tensor_scalar(A[:, i, 0:QR], MB[i][:, 0:QR], r, None, ALU.mult).then_inc(copied[i], 1)
                nb = QR // P
                for i in range(n):
                    yield
                    dve.wait_ge(t_filled, before("t_filled", "dq", g0) + i + 1)
                    nc.vector.tensor_tensor(TT[:, 0:nb, i * P:(i + 1) * P], T[:, 0:QR].rearrange(blocks, t=P),
                                            columns(G_Q, nb), ALU.mult).then_inc(t_copied, 1)

            def uqp_stage(g0, n):
                yield
                yield
                dve.wait_ge(weights_used, used("w_uq_pe", g0, 1))
                for i in range(n):
                    if i:
                        settle()
                        dve.wait_ge(copied[i - 1], before(("m_copied", "b_copied")[i - 1], "uqp", g0) + 1)
                    rope(qpe[i], MB[i][:, 0:H * ROPE], H, g0 % NC + i, rtmp).then_inc(copied[i], 1)

            def heads_stage(g, n):
                c = g % NC
                width = (c + 1) * P
                pair0 = c * HEAD_PAIRS

                def largest(k):
                    s = B[:, :].rearrange("p (e s) -> p e s", e=2)
                    m = c * H + 2 * k
                    dve.wait_ge(att_scored, pair0 + k + 1)
                    step(nc.vector.tensor_tensor(s[:, :, c * P:width], s[:, :, c * P:width],
                                                 mask.unsqueeze(1).broadcast_to([P, 2, P]), ALU.add))
                    settle()
                    step(nc.vector.reduce_max(amax[:, m:m + 2], s[:, :, 0:width], axis=AX))
                    settle()
                    nc.vector.tensor_scalar(nmax[:, m:m + 2], amax[:, m:m + 2], -SCALE, None, ALU.mult
                                            ).then_inc(att_maxed, 1)

                def diagonal(k):
                    m = c * H + 2 * k
                    dve.wait_ge(att_exped, m + 2)
                    step(nc.vector.reciprocal(arec[:, m:m + 2], asum[:, m:m + 2]))
                    settle()
                    if pair0 + k:
                        dve.wait_ge(att_turned, pair0 + k)
                    nc.vector.tensor_tensor(adiag, ident.unsqueeze(1).broadcast_to([P, 2, P]),
                                            arec[:, m:m + 2].unsqueeze(2).broadcast_to([P, 2, P]), ALU.mult
                                            ).then_inc(att_normed, 1)

                for part in range(HEAD_PAIRS + 2):
                    if part >= 2:
                        diagonal(part - 2)
                    if 1 <= part < HEAD_PAIRS + 1:
                        largest(part - 1)
                    yield

            def wo_stage(g0, n):
                for _ in range(4):
                    yield
                dve.wait_ge(weights_used, used("w_o", g0, 3))
                for i in range(n):
                    c = (g0 + i) % NC
                    nc.vector.tensor_tensor(X[:, c, :], X[:, c, :], MB[i][:, :], ALU.add).then_inc(x_ready, 1)

            def residual_stage(g, n):
                dve.wait_ge(acc_done, g + 1)
                dve.wait_ge(v_added, NDVE * (1 + (g + 1) * BODIES))
                nc.vector.tensor_tensor(X[:, g % NC, :], X[:, g % NC, :], acc[:, :], ALU.add).then_inc(x_ready, 1)
                yield

            def enorm_stage(g0, n):
                yield
                for i in range(n):
                    r = reciprocal_rms("enorm", g0, i)
                    nc.vector.tensor_scalar(A[:, i, :], X[:, (g0 + i) % NC, :], r, None, ALU.mult).then_inc(hat_ready, 1)
                for i in range(n):
                    yield
                    dve.wait_ge(t_filled, before("t_filled", "enorm", g0) + i + 1)
                    nc.vector.tensor_tensor(TT[:, :, i * P:(i + 1) * P], T[:, :].rearrange(blocks, t=P),
                                            columns(G_PLE + (g0 // NC) * DB, DB), ALU.mult).then_inc(t_copied, 1)

            def add_stage(g0, n):
                yield
                dve.wait_ge(weights_used, used("ple_wp", g0, 0))
                for i in range(n):
                    name = ("m_copied", "b_copied")[i]
                    dve.wait_ge(copied[i], before(name, "add", g0))
                    nc.vector.tensor_tensor(A[:, i, :], A[:, i, :], MB[i][:, :], ALU.mult).then_inc(copied[i], 1)
                for i in range(n):
                    c, name = (g0 + i) % NC, ("m_copied", "b_copied")[i]
                    dve.wait_ge(copied[i], before(name, "add", g0) + 1)
                    nc.vector.tensor_tensor(X[:, c, :], X[:, c, :], A[:, i, :], ALU.add).then_inc(x_ready, 1)
                if g0 >= NC:
                    yield
                    yield
                    if g0 == NC:
                        dve.wait_ge(gain_loaded, 32)
                    for i in range(n):
                        c = (g0 + i) % NC
                        r = reciprocal_rms("add", g0, i)
                        nc.vector.scalar_tensor_tensor(outs[c], X[:, c, :], r, gain[:, :], ALU.mult, ALU.mult
                                                       ).then_inc(out_ready, 1)

            stages = dict(pool=pool_stage, fnorm=fnorm_stage, asks0=lambda g, n: asks_stage(0, g, n),
                          asks1=lambda g, n: asks_stage(1, g, n), trig=trig_stage,
                          rank0=lambda g, n: rank_stage(0, g, n), rank1=lambda g, n: rank_stage(1, g, n),
                          latent=latent_stage, dq=dq_stage, uqp=uqp_stage, heads=heads_stage, wo=wo_stage,
                          residual=residual_stage, enorm=enorm_stage, add=add_stage)

            def gather_batches(g, u, end):
                Xc = X[:, g % NC, :]

                def batch(j, it, b):
                    first = g * BODIES + j
                    for s in range(b * BATCH, (b + 1) * BATCH):
                        dve.wait_ge(rows_loaded[s], it * 16 + 16 * (first + 1))
                        nc.vector.tensor_tensor_reduce(
                            out=slot[s][:, 0:D], in0=slot[s][:, 0:D], in1=HP[:, g % HPB, :], scale=1.0, scalar=0.0,
                            op0=ALU.mult, op1=ALU.add, accum_out=a[:, s:s + 1]).then_inc(dotted, 1)
                    at = slice(b * BATCH, (b + 1) * BATCH)
                    dve.wait_ge(gelued, it * NB + (first * NB + b + 1))
                    nc.vector.tensor_tensor(
                        w[:, at], act_a[:, at], gate[:, g % HPB, bass.ds(it * SLOTS + (j * SLOTS + b * BATCH), BATCH)],
                        ALU.mult).then_inc(weighted, 1)
                    dve.wait_ge(weighted, it * NB + (first * NB + b + 1))
                    for d, s in enumerate(DVE_SLOTS):
                        if s // BATCH == b:
                            dve.wait_ge(v_added, it * NDVE + (first * NDVE + NDVE + d))
                            nc.vector.scalar_tensor_tensor(Xc, slot[s][:, D:2 * D], w[:, s:s + 1], Xc,
                                                           ALU.mult, ALU.add).then_inc(v_added, 1)

                run_batches(dve, u, end, batch)

            nc.vector.memset(zeros[:], 0.0).then_inc(zeroed, 1)
            nc.vector.memset(w[:], 0.0).then_inc(v_added, NDVE)
            dve.wait_ge(cst_loaded, 16)
            dve.wait_ge(const_loaded, 16 * CONSTS)
            run_between(stages, gather_batches)


def shape_constants():
    t = np.arange(P)
    c = np.zeros((P, C_WIDTH), np.float32)
    c[:, C_IDENT:C_IDENT + P] = np.eye(P)
    c[:, C_MASK:C_MASK + P] = np.where(t[None, :] <= t[:, None], 0.0, -1.0e30)
    c[:, C_IOTA:C_IOTA + TOPK] = np.arange(TOPK)
    c[:, C_INV:C_INV + HALF] = np.float32(10000.0) ** (-np.arange(0, ROPE, 2, dtype=np.float32) / ROPE)
    c[:, C_EPS] = EPS
    pools = np.zeros((P, 3, len(WINDOWS), P), np.float32)
    for n, w in enumerate(WINDOWS):
        d = t[None, :] - t[:, None]
        inside = (d >= 0) & (d < w)
        pools[:, 0, n] = inside / np.minimum(t + 1, w)[None, :] - np.eye(P)
        pools[:, 1, n] = inside / w - np.eye(P)
        pools[:, 2, n] = (d + P < w) / w
    return c, pools.reshape(P, -1)


def by_columns(w, cols):
    k, n = w.shape
    return np.ascontiguousarray(w.reshape(k // P, P, n // cols, cols).transpose(2, 1, 0, 3).reshape(n // cols, P, -1))


def by_halves(w):
    return by_columns(w, 512).transpose(1, 0, 2).reshape(1, P, -1)


def kernel(x, p, positions, mix_norm, ffn_norm, pool_w, pool_scale, kv_in_norm, w_dkv, kv_norm, w_ukv,
           w_dq, q_norm, w_uq, w_o, peer_wq, peer_keys, peer_u, peer_v, ple_norm, ple_wg, ple_wp, final_norm):
    import concourse.bacc as bacc
    from concourse.bass_utils import run_bass_kernel_spmd as run

    (x, p, positions, mix_norm, ffn_norm, pool_w, pool_scale, kv_in_norm, w_dkv, kv_norm, w_ukv, w_dq, q_norm, w_uq,
     w_o, peer_wq, peer_keys, peer_u, peer_v, ple_norm, ple_wg, ple_wp, final_norm) = (
        np.asarray(v) for v in (
            x, p, positions, mix_norm, ffn_norm, pool_w, pool_scale, kv_in_norm, w_dkv, kv_norm, w_ukv, w_dq, q_norm,
            w_uq, w_o, peer_wq, peer_keys, peer_u, peer_v, ple_norm, ple_wg, ple_wp, final_norm))

    consts, pools = shape_constants()
    arrays = {
        "consts": consts,
        "pools": pools,
        "gcols": np.concatenate([v.reshape(-1, P).T for v in (kv_in_norm, mix_norm[1], ple_norm[0], ple_norm[1],
                                                              kv_norm, q_norm[0])], axis=1),
        "gains": np.stack([mix_norm[0], pool_scale[0], ffn_norm[0], ffn_norm[1], final_norm]),
        "positions": positions.reshape(NC, P).T,
        "x": x.reshape(S, D),
        "pT": p.reshape(DEPTH, S, PLE // P, P).transpose(0, 3, 2, 1),
    }
    for l in range(DEPTH):
        arrays[f"uv{l}"] = np.concatenate([peer_u[l], peer_v[l]], axis=1)
    heads_kv = w_ukv.reshape(KVR, H, NOPE + VH)
    heads_q = w_uq[0].reshape(QR, H, NOPE + ROPE)
    per_layer = {
        ("pool_w", 0): pool_w[0].reshape(len(WINDOWS), 2, P, GW).transpose(2, 0, 1, 3).reshape(1, P, -1),
        ("w_ukv_k", 1): by_columns(heads_kv[:, :, :NOPE].reshape(KVR, -1), H * NOPE),
        ("w_ukv_v", 1): by_halves(heads_kv[:, :, NOPE:].reshape(KVR, -1)),
        ("w_dq", 1): by_columns(w_dq[0], 256),
        ("w_uq_nope", 1): by_columns(heads_q[:, :, :NOPE].reshape(QR, -1), 256),
        ("w_uq_pe", 1): by_columns(heads_q[:, :, NOPE:].reshape(QR, -1), 256),
        ("w_o", 1): by_columns(w_o[0], 256),
    }
    for l in range(DEPTH):
        per_layer["wq", l] = by_columns(peer_wq[l], 256)
        arrays[f"keys{l}"] = peer_keys[l].reshape(2 * PH, P, P).transpose(2, 0, 1).reshape(P, DB, -1)
        per_layer["ple_wg", l] = by_columns(ple_wg[l], 256)
        per_layer["ple_wp", l] = by_halves(ple_wp[l])
    for (name, l), v in per_layer.items():
        arrays[f"{name}_{l}"] = v
    arrays["w_dkv_a"] = by_columns(w_dkv[:, :KVR], KVR)
    arrays["w_dkv_b"] = by_columns(w_dkv[:, KVR:], ROPE)
    arrays = {n: np.ascontiguousarray(v) for n, v in arrays.items()}

    nc = bacc.Bacc("TRN2", target_bir_lowering=False, num_devices=1)
    ap = {n: nc.dram_tensor(f"in_{n}", v.shape, mybir.dt.from_np(v.dtype), kind="ExternalInput").ap()
          for n, v in arrays.items()}
    out = nc.dram_tensor("out", (S, D), F32, kind="ExternalOutput").ap()
    weights = {(name, l): [ap[f"{name}_{l}"][i] for i in range(v.shape[0])] for (name, l), v in per_layer.items()}
    weights["w_dkv", 1] = [ap["w_dkv_a"][0], ap["w_dkv_b"][0]]
    trunk(nc, ap["consts"], ap["pools"], ap["gcols"], ap["gains"], ap["positions"], ap["x"], ap["pT"],
          [ap["uv0"], ap["uv1"]], weights, [ap["keys0"], ap["keys1"]], out)
    r = run(nc, [{f"in_{n}": v for n, v in arrays.items()}], core_ids=[0])
    return r.results[0]["out"].reshape(1, S, D)
```
